# Optimizing a Trainium2 kernel written in Bass

```python
import jax, jax.numpy as jnp
from jax import lax
import numpy as np

D_MODEL = 1024
BATCH = 1
SEQ = 512
DEPTH = 2

CTX_LEN = 256
GRID_W = 64

MIX_WIDTH = D_MODEL
CONV_CH = MIX_WIDTH // 4
CONV_K = 31
RET_HEADS = 4
RET_QK_DIM = 32
RET_V_DIM = 64
RET_CHUNK = 128
MLA_HEADS = 8
MLA_NOPE_DIM = 64
MLA_ROPE_DIM = 32
MLA_V_DIM = 64
MLA_Q_RANK = 256
MLA_KV_RANK = 128
Q_BLOCK = 128
ROPE_BASE = 10000.0
N_EXPERTS = 64
TOP_K = 6
EXPERT_DIM = 256
ROUTED_SCALE = 2.5
MOE_BLOCK = 128
NORM_EPS = 1e-6

IN_WIDTHS = (2 * CONV_CH,
             RET_HEADS * RET_QK_DIM, RET_HEADS * RET_QK_DIM, RET_HEADS * RET_V_DIM, RET_HEADS * RET_V_DIM,
             MLA_Q_RANK, MLA_KV_RANK, MLA_ROPE_DIM)
IN_SPLITS = tuple(sum(IN_WIDTHS[:i + 1]) for i in range(len(IN_WIDTHS) - 1))
IN_COLS = sum(IN_WIDTHS)

kernel_name = 'hybrid_conv_retention_mla_moe_dit'

def rms_norm(x, w):
    xf = x.astype(jnp.float32)
    y = xf * lax.rsqrt(jnp.mean(xf * xf, axis=-1, keepdims=True) + NORM_EPS)
    return y.astype(x.dtype) * w

def layer_norm(x, w, b):
    xf = x.astype(jnp.float32)
    mu = jnp.mean(xf, axis=-1, keepdims=True)
    var = jnp.mean(jnp.square(xf - mu), axis=-1, keepdims=True)
    return ((xf - mu) * lax.rsqrt(var + NORM_EPS)).astype(x.dtype) * w + b

def modulate(h, shift, scale):
    return h * (1 + scale) + shift

def axial_rope_tables(rows, dim):
    pos_r = jnp.repeat(jnp.arange(rows, dtype=jnp.float32), GRID_W)
    pos_c = jnp.tile(jnp.arange(GRID_W, dtype=jnp.float32), rows)
    n_freq = dim // 4
    inv = ROPE_BASE ** (-jnp.arange(n_freq, dtype=jnp.float32) / n_freq)
    ang = jnp.concatenate([pos_r[:, None] * inv, pos_c[:, None] * inv], axis=-1)
    return jnp.cos(ang), jnp.sin(ang)

def apply_rope(x, cos, sin):
    x1, x2 = jnp.split(x, 2, axis=-1)
    cos = cos.astype(x.dtype)
    sin = sin.astype(x.dtype)
    return jnp.concatenate([x1 * cos - x2 * sin, x1 * sin + x2 * cos], axis=-1)

def conformer_conv(u, conv_w, conv_b, ln_w, ln_b):
    a, g = jnp.split(u, 2, axis=-1)
    h = a * jax.nn.sigmoid(g)
    h = lax.conv_general_dilated(h, conv_w[:, None, :], window_strides=(1,),
                                 padding=[(CONV_K // 2, CONV_K // 2)],
                                 dimension_numbers=('NWC', 'WIO', 'NWC'),
                                 feature_group_count=CONV_CH) + conv_b
    return jax.nn.silu(layer_norm(h, ln_w, ln_b))

def retention_scan(q, k, v, log_gamma, s0):
    b, n_tok, h, dk = q.shape
    dv = v.shape[-1]
    n_chunks = n_tok // RET_CHUNK

    def to_chunks(t):
        return t.reshape(b, n_chunks, RET_CHUNK, h, t.shape[-1]).transpose(1, 0, 3, 2, 4)

    idx = jnp.arange(RET_CHUNK, dtype=jnp.float32)
    rel = idx[:, None] - idx[None, :]
    decay_in = jnp.where(rel >= 0, jnp.exp(log_gamma[:, None, None] * jnp.maximum(rel, 0.0)), 0.0)
    decay_q = jnp.exp(log_gamma[:, None] * (idx + 1.0))[:, :, None]
    decay_k = jnp.exp(log_gamma[:, None] * (RET_CHUNK - 1.0 - idx))[:, :, None]
    decay_chunk = jnp.exp(log_gamma * RET_CHUNK)[:, None, None]

    def step(s, qkv):
        qc, kc, vc = qkv
        inner = jnp.einsum('bhqd,bhkd->bhqk', qc, kc) * decay_in
        y = (jnp.einsum('bhqk,bhkv->bhqv', inner, vc)
             + jnp.einsum('bhqd,bhdv->bhqv', qc * decay_q, s))
        s = s * decay_chunk + jnp.einsum('bhkd,bhkv->bhdv', kc * decay_k, vc)
        return s, y

    s_final, ys = lax.scan(step, s0, (to_chunks(q), to_chunks(k), to_chunks(v)))
    return ys.transpose(1, 0, 3, 2, 4).reshape(b, n_tok, h, dv), s_final

def retention_qkv(zq, zk, zv, rope):
    b, n_tok, _ = zq.shape
    q = zq.reshape(b, n_tok, RET_HEADS, RET_QK_DIM).astype(jnp.float32)
    k = zk.reshape(b, n_tok, RET_HEADS, RET_QK_DIM).astype(jnp.float32) * (RET_QK_DIM ** -0.5)
    v = zv.reshape(b, n_tok, RET_HEADS, RET_V_DIM).astype(jnp.float32)
    if rope is not None:
        cos, sin = rope
        q = apply_rope(q, cos[None, :, None, :], sin[None, :, None, :])
        k = apply_rope(k, cos[None, :, None, :], sin[None, :, None, :])
    return q, k, v

def retention_out(y, g, gn_w):
    b, n_tok, h, dv = y.shape
    mu = jnp.mean(y, axis=-1, keepdims=True)
    var = jnp.mean(jnp.square(y - mu), axis=-1, keepdims=True)
    yn = ((y - mu) * lax.rsqrt(var + NORM_EPS)).reshape(b, n_tok, h * dv).astype(g.dtype)
    return jax.nn.silu(g) * (yn * gn_w)

def mla_q(cq, q_norm_w, w_uq, rope):
    b, n_tok, _ = cq.shape
    q = (rms_norm(cq, q_norm_w) @ w_uq).reshape(b, n_tok, MLA_HEADS, MLA_NOPE_DIM + MLA_ROPE_DIM)
    if rope is not None:
        cos, sin = rope
        q = jnp.concatenate([q[..., :MLA_NOPE_DIM],
                             apply_rope(q[..., MLA_NOPE_DIM:], cos[None, :, None, :], sin[None, :, None, :])], axis=-1)
    return q

def mla_kv(ckv, k_rope, kv_norm_w, w_ukv, rope):
    b, n_tok, _ = ckv.shape
    kv = (rms_norm(ckv, kv_norm_w) @ w_ukv).reshape(b, n_tok, MLA_HEADS, MLA_NOPE_DIM + MLA_V_DIM)
    k_nope, v = kv[..., :MLA_NOPE_DIM], kv[..., MLA_NOPE_DIM:]
    if rope is not None:
        cos, sin = rope
        k_rope = apply_rope(k_rope, cos[None], sin[None])
    k = jnp.concatenate([k_nope, jnp.broadcast_to(k_rope[:, :, None, :], (b, n_tok, MLA_HEADS, MLA_ROPE_DIM))], axis=-1)
    return k, v

def block_attention(q, k, v):
    b, n_q, h, dq = q.shape
    n_blocks = n_q // Q_BLOCK
    scale = dq ** -0.5
    qb = q.reshape(b, n_blocks, Q_BLOCK, h, dq).swapaxes(0, 1)

    def one_block(qi):
        s = jnp.einsum('bqhd,bkhd->bhqk', qi, k).astype(jnp.float32) * scale
        p = jax.nn.softmax(s, axis=-1).astype(v.dtype)
        return jnp.einsum('bhqk,bkhd->bqhd', p, v)

    o = lax.map(one_block, qb)
    return o.swapaxes(0, 1).reshape(b, n_q, h * v.shape[-1])

def token_mixer(hl, hc, w_in, conv_w, conv_b, conv_ln_w, conv_ln_b, ret_decay_logit, ret_gn_w,
                q_norm_w, w_uq, kv_norm_w, w_ukv, w_out, rope_ret, rope_mla, with_ctx_out):
    zl = jnp.split(hl @ w_in, IN_SPLITS, axis=-1)
    zc = jnp.split(hc @ w_in, IN_SPLITS, axis=-1)

    conv_l = conformer_conv(zl[0], conv_w, conv_b, conv_ln_w, conv_ln_b)

    ql, kl, vl = retention_qkv(zl[1], zl[2], zl[3], rope_ret)
    qc, kc, vc = retention_qkv(zc[1], zc[2], zc[3], None)
    log_gamma = jax.nn.log_sigmoid(ret_decay_logit.astype(jnp.float32))
    s0 = jnp.zeros((hl.shape[0], RET_HEADS, RET_QK_DIM, RET_V_DIM), jnp.float32)
    flip = lambda t: t[:, ::-1]
    yc_f, sc_f = retention_scan(qc, kc, vc, log_gamma[0], s0)
    yc_b, sc_b = retention_scan(flip(qc), flip(kc), flip(vc), log_gamma[1], s0)
    yl_f, _ = retention_scan(ql, kl, vl, log_gamma[0], sc_f)
    yl_b, _ = retention_scan(flip(ql), flip(kl), flip(vl), log_gamma[1], sc_b)
    ret_l = retention_out(yl_f + flip(yl_b), zl[4], ret_gn_w)

    k_ctx, v_ctx = mla_kv(zc[6], zc[7], kv_norm_w, w_ukv, None)
    k_lat, v_lat = mla_kv(zl[6], zl[7], kv_norm_w, w_ukv, rope_mla)
    q_lat = mla_q(zl[5], q_norm_w, w_uq, rope_mla)
    mla_l = block_attention(q_lat, jnp.concatenate([k_ctx, k_lat], axis=1), jnp.concatenate([v_ctx, v_lat], axis=1))

    yl = jnp.concatenate([conv_l, ret_l, mla_l], axis=-1) @ w_out
    if not with_ctx_out:
        return yl, None
    conv_c = conformer_conv(zc[0], conv_w, conv_b, conv_ln_w, conv_ln_b)
    ret_c = retention_out(yc_f + flip(yc_b), zc[4], ret_gn_w)
    mla_c = block_attention(mla_q(zc[5], q_norm_w, w_uq, None), k_ctx, v_ctx)
    yc = jnp.concatenate([conv_c, ret_c, mla_c], axis=-1) @ w_out
    return yl, yc

def swiglu(h, w_gate, w_up, w_down):
    return (jax.nn.silu(h @ w_gate) * (h @ w_up)) @ w_down

def routed_experts(h, expert_idx, expert_w, e_gate, e_up, e_down):
    n_tok, d = h.shape
    n_assign = n_tok * TOP_K
    n_blocks = -(-n_assign // MOE_BLOCK) + N_EXPERTS
    flat_e = expert_idx.reshape(-1)
    flat_tok = jnp.repeat(jnp.arange(n_tok, dtype=jnp.int32), TOP_K)
    flat_w = expert_w.reshape(-1)
    order = jnp.argsort(flat_e)
    sorted_e = flat_e[order]
    counts = jnp.bincount(flat_e, length=N_EXPERTS)
    padded = (counts + MOE_BLOCK - 1) // MOE_BLOCK * MOE_BLOCK
    pad_end = jnp.cumsum(padded)
    pad_start = pad_end - padded
    start = jnp.cumsum(counts) - counts
    dest = pad_start[sorted_e] + jnp.arange(n_assign, dtype=jnp.int32) - start[sorted_e]
    slot_tok = jnp.full((n_blocks * MOE_BLOCK,), n_tok, jnp.int32).at[dest].set(flat_tok[order])
    slot_w = jnp.zeros((n_blocks * MOE_BLOCK,), h.dtype).at[dest].set(flat_w[order])
    block_e = jnp.minimum(jnp.searchsorted(pad_end, jnp.arange(n_blocks, dtype=jnp.int32) * MOE_BLOCK, side='right'),
                          N_EXPERTS - 1)
    h_pad = jnp.concatenate([h, jnp.zeros((1, d), h.dtype)], axis=0)

    def step(y, blk):
        tok, wt, e = blk
        out = swiglu(h_pad[tok], e_gate[e], e_up[e], e_down[e])
        return y.at[tok].add(out * wt[:, None]), None

    y, _ = lax.scan(step, jnp.zeros((n_tok + 1, d), h.dtype),
                    (slot_tok.reshape(n_blocks, MOE_BLOCK), slot_w.reshape(n_blocks, MOE_BLOCK), block_e))
    return y[:n_tok]

def moe_ffn(h, router_w, router_b, e_gate, e_up, e_down, s_gate, s_up, s_down):
    scores = jax.nn.sigmoid((h @ router_w).astype(jnp.float32))
    _, idx = lax.top_k(scores + router_b.astype(jnp.float32), TOP_K)
    w = jnp.take_along_axis(scores, idx, axis=-1)
    w = (w / jnp.sum(w, axis=-1, keepdims=True) * ROUTED_SCALE).astype(h.dtype)
    return routed_experts(h, idx, w, e_gate, e_up, e_down) + swiglu(h, s_gate, s_up, s_down)

def setup_inputs(seed: int = 0) -> dict:
    key = jax.random.key(seed)
    ks = jax.random.split(key, 32)
    f32 = jnp.float32
    nrm = lambda k, shape, scale: jax.random.normal(k, shape, f32) * scale
    gain = lambda k, shape: 1.0 + 0.02 * jax.random.normal(k, shape, f32)
    ret_logit0 = jnp.log(2.0 ** (5.0 + jnp.arange(RET_HEADS, dtype=f32)) - 1.0)
    return {
        'x': nrm(ks[0], (BATCH, SEQ, D_MODEL), 1.0),
        'c': nrm(ks[1], (BATCH, D_MODEL), 1.0),
        'ctx': nrm(ks[2], (BATCH, CTX_LEN, D_MODEL), 1.0),
        'c_ctx': nrm(ks[3], (D_MODEL,), 1.0),
        'mod_w': nrm(ks[4], (DEPTH, D_MODEL, 6 * D_MODEL), 0.5 * D_MODEL ** -0.5),
        'mod_b': nrm(ks[5], (DEPTH, 6 * D_MODEL), 0.02),
        'norm1_w': gain(ks[6], (DEPTH, D_MODEL)),
        'w_in': nrm(ks[7], (DEPTH, D_MODEL, IN_COLS), D_MODEL ** -0.5),
        'conv_w': nrm(ks[8], (DEPTH, CONV_K, CONV_CH), CONV_K ** -0.5),
        'conv_b': nrm(ks[9], (DEPTH, CONV_CH), 0.02),
        'conv_ln_w': gain(ks[10], (DEPTH, CONV_CH)),
        'conv_ln_b': nrm(ks[11], (DEPTH, CONV_CH), 0.02),
        'ret_decay_logit': ret_logit0 + 0.1 * jax.random.normal(ks[12], (DEPTH, 2, RET_HEADS), f32),
        'ret_gn_w': gain(ks[13], (DEPTH, RET_HEADS * RET_V_DIM)),
        'q_norm_w': gain(ks[14], (DEPTH, MLA_Q_RANK)),
        'w_uq': nrm(ks[15], (DEPTH, MLA_Q_RANK, MLA_HEADS * (MLA_NOPE_DIM + MLA_ROPE_DIM)), MLA_Q_RANK ** -0.5),
        'kv_norm_w': gain(ks[16], (DEPTH, MLA_KV_RANK)),
        'w_ukv': nrm(ks[17], (DEPTH, MLA_KV_RANK, MLA_HEADS * (MLA_NOPE_DIM + MLA_V_DIM)), MLA_KV_RANK ** -0.5),
        'w_out': nrm(ks[18], (DEPTH, MIX_WIDTH, D_MODEL), MIX_WIDTH ** -0.5),
        'norm2_w': gain(ks[19], (DEPTH, D_MODEL)),
        'router_w': nrm(ks[20], (DEPTH, D_MODEL, N_EXPERTS), D_MODEL ** -0.5),
        'router_b': nrm(ks[21], (DEPTH, N_EXPERTS), 0.01),
        'exp_w_gate': nrm(ks[22], (DEPTH, N_EXPERTS, D_MODEL, EXPERT_DIM), D_MODEL ** -0.5),
        'exp_w_up': nrm(ks[23], (DEPTH, N_EXPERTS, D_MODEL, EXPERT_DIM), D_MODEL ** -0.5),
        'exp_w_down': nrm(ks[24], (DEPTH, N_EXPERTS, EXPERT_DIM, D_MODEL), EXPERT_DIM ** -0.5),
        'sh_w_gate': nrm(ks[25], (DEPTH, D_MODEL, EXPERT_DIM), D_MODEL ** -0.5),
        'sh_w_up': nrm(ks[26], (DEPTH, D_MODEL, EXPERT_DIM), D_MODEL ** -0.5),
        'sh_w_down': nrm(ks[27], (DEPTH, EXPERT_DIM, D_MODEL), EXPERT_DIM ** -0.5),
        'final_norm_w': gain(ks[28], (D_MODEL,)),
    }

def reference(x, c, ctx, c_ctx, mod_w, mod_b, norm1_w, w_in, conv_w, conv_b, conv_ln_w, conv_ln_b,
              ret_decay_logit, ret_gn_w, q_norm_w, w_uq, kv_norm_w, w_ukv, w_out, norm2_w,
              router_w, router_b, exp_w_gate, exp_w_up, exp_w_down, sh_w_gate, sh_w_up, sh_w_down,
              final_norm_w):
    b, n_lat, d = x.shape
    n_ctx = ctx.shape[1]
    rows = n_lat // GRID_W
    rope_ret = axial_rope_tables(rows, RET_QK_DIM)
    rope_mla = axial_rope_tables(rows, MLA_ROPE_DIM)
    xl, xc = x, ctx
    for i in range(DEPTH):
        last = i == DEPTH - 1
        mod_l = jax.nn.silu(c) @ mod_w[i] + mod_b[i]
        mod_c = jax.nn.silu(c_ctx) @ mod_w[i] + mod_b[i]
        sh1, sc1, g1, sh2, sc2, g2 = jnp.split(mod_l[:, None, :], 6, axis=-1)
        csh1, csc1, cg1, csh2, csc2, cg2 = jnp.split(mod_c, 6)

        hl = modulate(rms_norm(xl, norm1_w[i]), sh1, sc1)
        hc = modulate(rms_norm(xc, norm1_w[i]), csh1, csc1)
        yl, yc = token_mixer(hl, hc, w_in[i], conv_w[i], conv_b[i], conv_ln_w[i], conv_ln_b[i],
                             ret_decay_logit[i], ret_gn_w[i], q_norm_w[i], w_uq[i], kv_norm_w[i], w_ukv[i],
                             w_out[i], rope_ret, rope_mla, not last)
        xl = xl + g1 * yl

        hl2 = modulate(rms_norm(xl, norm2_w[i]), sh2, sc2).reshape(b * n_lat, d)
        if last:
            out = moe_ffn(hl2, router_w[i], router_b[i], exp_w_gate[i], exp_w_up[i], exp_w_down[i],
                          sh_w_gate[i], sh_w_up[i], sh_w_down[i])
            xl = xl + g2 * out.reshape(b, n_lat, d)
        else:
            xc = xc + cg1 * yc
            hc2 = modulate(rms_norm(xc, norm2_w[i]), csh2, csc2).reshape(b * n_ctx, d)
            out = moe_ffn(jnp.concatenate([hl2, hc2], axis=0), router_w[i], router_b[i], exp_w_gate[i],
                          exp_w_up[i], exp_w_down[i], sh_w_gate[i], sh_w_up[i], sh_w_down[i])
            xl = xl + g2 * out[:b * n_lat].reshape(b, n_lat, d)
            xc = xc + cg2 * out[b * n_lat:].reshape(b, n_ctx, d)
    return rms_norm(xl, final_norm_w)


_drawn_inputs = setup_inputs


def setup_inputs(seed=0):
    import zlib

    import numpy as np

    out = dict(_drawn_inputs(seed))
    spreads = {}
    factors = {'conv_ln_w': 3.035,
     'conv_ln_b': 3.072,
     'ret_gn_w': 3.146,
     'q_norm_w': 5.04,
     'kv_norm_w': 3.498,
     'final_norm_w': 2.743}
    for name, (base, spread) in spreads.items():
        noise = np.random.default_rng([zlib.crc32(name.encode()), seed]).standard_normal(out[name].shape)
        drawn = base * np.exp(spread * noise) if base else spread * noise
        out[name] = __import__('jax').numpy.asarray(drawn.astype(out[name].dtype))
    for name, factor in factors.items():
        out[name] = (out[name] * factor).astype(out[name].dtype)
    return out
```

```python
import math
from contextlib import ExitStack

import numpy as np
import concourse.bass as bass
from concourse import mybir

F32 = mybir.dt.float32
I32 = mybir.dt.int32
U32 = mybir.dt.uint32
ALU = mybir.AluOpType
ACT = mybir.ActivationFunctionType
AX = mybir.AxisListType.X

P = 128
D = 1024
KC = D // P
LAYERS = 2
LAT, CTX = 512, 256
TOK = LAT + CTX
SEG = ((0, LAT), (LAT, CTX))
EPS = 1e-6
CK = 31
HEADS_R, DK_R, DV_R = 4, 32, 64
HEADS, NOPE, ROPE, DV = 8, 64, 32, 64
QK = NOPE + ROPE
EXPERTS, TOPK, FE = 64, 6, 256
ROUTED_SCALE = 2.5
MOD = 6 * KC
WEXP = KC * 2 * FE + (FE // P) * D
SLOTS = 3
BLOCKS = 106
BIG = 1 << 20
PADW = 15 + LAT + 30 + CTX + 15
PADAT = (15, 15 + LAT + 30)

PAR = {}
_at = 0
for _n, _w in (("mod_b", 96), ("n1", 16), ("n2", 16), ("conv_w", 2 * CK), ("conv_b", 2), ("ln_w", 2), ("ln_b", 2),
               ("gn_w", 2), ("qn", 2), ("kvn", 1), ("decay", 8), ("router_b", 64), ("router_w", KC * EXPERTS),
               ("final", KC)):
    PAR[_n] = (_at, _w)
    _at += _w
NPAR = _at
CON = {}
_at = 0
for _n, _w in (("ident", P), ("perm", P), ("headavg", P), ("tri", P), ("inv1024", P), ("inv256", P), ("inv128", P),
               ("ones", P), ("cos", LAT), ("sin", LAT), ("headmask", HEADS_R), ("iota64", EXPERTS), ("iota128", P), ("fold", EXPERTS), ("fold4", ROPE)):
    CON[_n] = (_at, _w)
    _at += _w
NCON = _at
STRIP_A, STRIP_B = 896, 640


SQUARES = {"n1": KC, "n2": KC, "nf": 2, "cv": 2, "cqn": 2, "ckvn": 1, "gv": 1}


class Plan:

    def __init__(self, l):
        sq = (0, 1) if l == 0 else (0,)
        t_out = 6 if l == 0 else 4
        steps, later = [], []
        if l == 0:
            for k in range(KC):
                if k in (4, 6):
                    steps.append(("n1", k // 2 - 2))
                steps.append(("mod", 0, 0, k))
            steps += [("md", 0, 0), ("mt", 0, 0)]
            later = [("mod", lm, r, k) for lm, r in [(0, 1), (0, 2)] + [(lm, r) for lm in range(1, LAYERS) for r in range(3)]
                     for k in range(KC)]

        def fill(n):
            for _ in range(min(n, len(later))):
                g = later.pop(0)
                steps.append(g)
                if g[3] == KC - 1:
                    steps.extend([("md",) + g[1:3], ("mt",) + g[1:3]])

        if l:
            steps += [("n1", 0), ("n1", 1)]
        steps.append(("shift",))
        zs = [[(n, b, s) for s in sq for n in ("g", "a")] for b in range(2)]
        zs += [[("rq", s) for s in sq] + [("rk", s) for s in (0, 1)], [("rv", t) for t in range(6)]]
        zs += [[(n, b, s) for b in range(2) for s in sq] for n in ("rg", "cq")]
        zs += [[("ckv", s) for s in (0, 1)] + [("kr", s) for s in (0, 1)]]
        for i, group in enumerate(zs):
            steps.append(("in", i))
            for z in group:
                steps.append(z)
                fill(2 if z[0] != "rv" and z[-1] == 0 else 1)
                if z == ("cq", 1, sq[-1]):
                    steps += [("rot", "q"), ("rot", "k")] + [("cm", s) for s in sq]
                if z[0] == "ckv" and z[1] in sq:
                    steps.append(("cv", z[1]))
        fill(len(later))
        self.steps = steps
        self.loads = []
        for g in steps:
            if g[0] == "mod":
                self.loads.append(g)
            elif g[0] == "in":
                self.loads += [("in", i) for i in ((0, 1) if g[1] == 0 else (g[1] + 1,)) if i < len(zs)]
        self.loads += [("out", i) for i in range(KC // 2)]
        j = [(x, "D" if x[0] in ("a", "rot", "cm") else "A") for x in steps if x[0] not in ("mod", "in", "shift")]
        j += [(("kf", s), "A") for s in (0, 1)] + [(("rot", "kr"), "D")]
        j += [(("cqn", s), "A") for s in sq] + [(("ckvn", s), "A") for s in (0, 1)]
        self.before_retention = len(j)
        halves = [(b, s) for b in range(2) for s in sq]
        j += [(("gm", b, s), "D") for b, s in halves]
        for i in range(4):
            j += [(("qn", i, 0), "A")]
            j += [(("gv",) + halves[i], "A")] if i < len(halves) else []
        j += [(("qr", r, 0), "A") for r in range(2)] + [(("rot2", r), "D") for r in range(2)]
        for s in sq[1:]:
            j += [(("qn", i, s), "A") for i in range(4)] + [(("qr", r, s), "A") for r in range(2)]
        self.halves = halves
        j += [(("vm", t), "A") for t in range(6)]
        j += [(("kn", i, s), "AD"[i % 2]) for s in (0, 1) for i in range(4)]
        self.before_attention = len(j)
        j += [(("wo", m, s), "D") for m in range(KC) for s in sq]
        j += [(("n2", s), "A") for s in sq]
        j += [(("rl", s), "A") for s in sq] + [("router", "A")]
        for s in sq:
            j += [(("sg", 0, s), "A"), (("su", 0, s), "D")]
            j += [("cum", "D"), ("sum", "D"), ("cnt", "D")] if s == 0 else []
            j += [(("sg", 1, s), "A")]
            j += [("start", "D"), ("eid", "D")] if s == 0 else []
            j += [(("su", 1, s), "D")]
            if s == 0:
                j += [(("hr", t, i), "A") for t in range(t_out) for i in range(2)]
            j += [(("sd", m, s), "D") for m in range(KC)]
        self.before_experts = len(j)
        for t in range(t_out):
            j += [(("ct", t, i), "D") for i in range(2)]
            if l == LAYERS - 1:
                j += [(("nf", t), "A")]
        self.jobs = j
        self.number = {k: n for n, (k, _) in enumerate(j)}
        count = {"A": 0, "D": 0}
        self.evac = {}
        self.square, self.done, n, plain = {}, {}, 0, 0
        for k, e in j:
            count[e] += 1
            self.evac[k] = (e, count[e])
            c = SQUARES.get(k[0], 0)
            if k[0] == "md":
                self.done[k] = ("mod_used", KC * (1 + sum(x[0] == "md" for x in self.done)))
                continue
            if c:
                self.square[k] = (n, c)
                n += c
                self.done[k] = ("sq_used", n)
            else:
                plain += 1
                self.done[k] = ("pe_jobs", plain)
        self.norm = {k: i for i, k in enumerate(self.square)}
        self.sq, self.t_out = sq, t_out
        self.bank, self.bank_before, held, turn = {}, {}, {}, 0
        for i, (k, _) in enumerate(j):
            if k[0] == "md":
                bk = 7
            else:
                bk, turn = (turn % 7, turn + 1) if i < self.before_retention else (i % 8, turn)
            self.bank[k] = bk
            self.bank_before[k] = held.get(bk)
            held[bk] = k
        last = sq[-1]
        self.last_user = {("in", i): k for i, k in enumerate([("a", 0, last), ("a", 1, last), ("rk", 1), ("rv", 5),
                                                              ("rg", 1, last), ("cq", 1, last), ("kr", 1)])}
        self.last_user.update({("out", i): ("wo", 2 * i + 1, last) for i in range(KC // 2)})


def hybrid_backbone(nc, A, out):
    ctx = ExitStack()
    with ctx:
        def sb(name, shape, dt=F32):
            return ctx.enter_context(nc.sbuf_tensor(name, shape, dt))

        sems = {}

        def sem(name):
            if name not in sems:
                sems[name] = ctx.enter_context(nc.semaphore(name.replace(" ", "_")))
            return sems[name]

        arena = sb("arena", [P, 44152 + 4096])

        def view(at, *shape, parts=P):
            n = int(np.prod(shape))
            v = arena[0:parts, at:at + n]
            if len(shape) == 2:
                v = v.rearrange("p (a b) -> p a b", a=shape[0])
            elif len(shape) == 3:
                v = v.rearrange("p (a b c) -> p a b c", a=shape[0], b=shape[1])
            return v

        X = view(0, KC, TOK)
        H = view(6144, KC, TOK)
        CAT = view(12288, KC, TOK)
        RING = view(18432, 2, 2, D)
        MODW = [view(at, 4, 512) for at in (22528, 24576, 26624)]
        WUQ = view(26624, 2, HEADS * QK)
        WUKV = view(28160, HEADS * (NOPE + DV))
        HPAD = view(29184, 2, PADW)
        MID = 30840
        RQ, RK = view(MID, TOK), view(MID + 768, TOK)
        RV = view(MID + 1536, 6, HEADS_R * DV_R)
        SA = view(MID + 3072, HEADS_R, STRIP_A)
        QM = H[:, 4:8, :]
        SB = view(MID + 6656, HEADS_R, STRIP_B)
        PB = view(MID + 9216, 4, 512)
        EX = view(MID + 9216, 2, STRIP_A)
        DTAB = view(MID + 11264, STRIP_A)
        DPOS = view(MID + 12160, STRIP_A)
        DNEG = view(12288 + 4 * TOK, STRIP_A)
        TMP = view(MID + 10240, 512)
        SQR = view(MID + 9216, 2, 512)
        SGS = view(MID + 7680, 2, 512)
        KALL = view(6144, HEADS, TOK)
        QALL = view(MID, HEADS, TOK)
        VM = view(MID + 6144, 6, HEADS * DV)
        PR = view(MID + 9216, 2, TOK)
        PT = view(MID + 10752, 2, TOK)
        OB = view(MID + 12288, 2, HEADS * DV)
        WB = view(12288, SLOTS, WEXP)
        HROW = view(MID, SLOTS, D)
        HT = view(MID + 3072, SLOTS, KC, P)
        AT = view(MID + 6144, SLOTS, 2, P)
        SG = view(MID + 6912, SLOTS, 2, P)
        YB = view(MID + 7680, SLOTS, D)
        ASH = view(MID + 10752, 2, TOK)
        LOGIT = view(MID + 9216, TOK)
        SC = view(MID + 12288, 6, EXPERTS)
        Y6 = arena[:, 12288:12288 + 3 * TOPK * D].rearrange("p (u k d) -> p u k d", u=3, k=TOPK)
        SQB = view(44152, 3, 512)
        MROW = view(45688, 512)
        RSB = view(46200, 4, 512)

        con = sb("con", [P, NCON])
        par = sb("par", [P, NPAR])
        silc = sb("silc", [P, KC, 2])
        modTs = [sb(f"modT{l}", [P, MOD, 2]) for l in range(LAYERS)]
        A1, A2 = sb("A1", [P, KC, 2]), sb("A2", [P, KC, 2])
        lg = sb("lg", [P, 12, 8])
        mx, nm = sb("mx", [P, 4]), sb("nm", [P, 4])
        rsum, rinv = sb("rsum", [P, 2, HEADS]), sb("rinv", [P, 2, HEADS])
        MSK = view(MID + 3072, 6, EXPERTS)
        ROWP = view(MID + 3456, 6, EXPERTS)
        QUO = view(MID + 2432, 6, EXPERTS)
        CNT = sb("CNT", [P, 4, EXPERTS])
        col = sb("col", [EXPERTS, 4])
        ncb = view(MID + 8704, P, parts=EXPERTS)
        endge = view(MID + 8832, P, parts=EXPERTS)
        rt = sb("rt", [P, 6, 5, 8])
        rtu = sb("rtu", [P, 6, 8], U32)
        dsti = sb("dsti", [P, 6, 8], I32)
        PAY = sb("PAY", [P, 6, TOPK, 4], I32)
        TAB = sb("TAB", [P, BLOCKS, 4], I32)
        GIX = sb("GIX", [P, SLOTS, 4], I32)
        SIX = sb("SIX", [P, SLOTS, 4], I32)
        PAYF = PAY[:, :, :, :].bitcast(F32)
        OH = view(MID + 4224, 6 * TOPK, EXPERTS)
        PICK = view(MID + 6528, 3 * TOPK, EXPERTS)
        SUMS = view(MID + 2048, 6, EXPERTS)
        epsb = sb("epsb", [P, 1])
        eids = sb("eids", [1, P], I32)
        meta = sb("meta", [1, 4], I32)
        metaf = view(MID + 8960, P + 8, parts=1)

        psum = ctx.enter_context(nc.psum_tensor("psum", [P, 8, 512], F32))

        def c(name, parts=P):
            a, w = CON[name]
            return con[0:parts, a:a + w]

        def pr(l, name, i=None):
            a, w = PAR[name]
            return par[:, a:a + w] if i is None else par[:, a + i:a + i + 1]

        plans = [Plan(l) for l in range(LAYERS)]
        ident = c("ident")
        hrows = [nc.dram_tensor(f"hrows{l}", (plans[l].t_out * P, D), F32, kind="Internal").ap() for l in range(LAYERS)]
        y6d = [nc.dram_tensor(f"y6_{l}", (TOPK * plans[l].t_out * P, D), F32, kind="Internal").ap() for l in range(LAYERS)]
        tabd = [nc.dram_tensor(f"table{l}", (P * BLOCKS, 4), I32, kind="Internal").ap() for l in range(LAYERS)]

        def job(l, key, n=512, parts=P):
            return psum[0:parts, plans[l].bank[key], 0:n]


        def ready(eng, l, key):
            s, n = plans[l].done[key]
            eng.wait_ge(sem(s if s == "mod_used" else f"{s}{l}"), n)

        def evacuated(eng, l, key):
            e, n = plans[l].evac[key]
            eng.wait_ge(sem(f"evac{e}{l}"), n)

        def ret_units(l):
            return [(s, 2 * b + h, kt) for s in plans[l].sq for b in range(HEADS_R // 2)
                    for kt in (range(6) if s == 0 else (4, 5)) for h in range(2)]

        def attn_units(l):
            return [(qt, h) for qt in range(plans[l].t_out) for h in range(HEADS)]

        def parts(sq):
            return [(s, a, CTX) for s in sq for a in range(SEG[s][0], SEG[s][0] + SEG[s][1], CTX)]

        def chain(eng, s):
            n = [0]

            def link(ins):
                n[0] += 1
                ins.then_inc(s, 1)
                eng.wait_ge(s, n[0])
            return link

        loads = [(l,) + g for l in range(LAYERS) for g in plans[l].loads]
        mods = [g for g in loads if g[1] == "mod"]
        weights = [g for g in loads if g[1] != "mod"]
        block = ctx.enter_context(nc.Block())

        @block.sync
        def _(sp):
            def load_weights(gs):
                for g in gs:
                    l = g[0]
                    if g[1] == "mod":
                        _, _, lm, r, k = g
                        n = mods.index(g)
                        if n >= 3:
                            sp.wait_ge(sem("mod_used"), n - 2)
                        sp.dma_start(MODW[n % 3].rearrange("p a b -> p (a b)"), A["mod_w"][lm, k * P:(k + 1) * P, r * 2048:(r + 1) * 2048]
                                     ).then_inc(sem(f"mod{n % 3}"), 16)
                        continue
                    n = weights.index(g)
                    if n >= 2:
                        old = weights[n - 2]
                        ready(sp, old[0], plans[old[0]].last_user[old[1:]])
                    sp.dma_start(RING[:, n % 2, :, :].rearrange("p a n -> p (a n)"),
                                 A["wblk"][l, g[2] + (0 if g[1] == "in" else 7)].rearrange("p a n -> p (a n)")
                                 ).then_inc(sem(f"ring{n % 2}"), 16)

            def load_expert(l, b, e):
                sp.dma_start(WB[:, b, :], A["experts"][bass.ds(e + l * EXPERTS, 1), :, :].rearrange(
                    "o p n -> (o p) n")).then_inc(sem(f"wexp{b}_{l}"), 16)

            def load_parameters(l):
                sp.dma_start(par[:, :], A["par"][l]).then_inc(sem("par_in"), 16)
                sp.dma_start(PAY[:, :, :, :], A["pay"][l]).then_inc(sem("pay_in"), 16)
                sp.dma_start(DTAB, A["dtab"]).then_inc(sem("dtab_in"), 16)

            sp.dma_start(silc[:, :, :], A["cc"]).then_inc(sem("cc_in"), 16)
            load_weights(loads[0:2])
            sp.dma_start(con[:, :], A["con"]).then_inc(sem("con_in"), 16)
            sp.dma_start(X[:, :, :], A["xT"]).then_inc(sem("x_in"), 16)
            load_weights(loads[2:5])
            load_parameters(0)
            load_weights(loads[5:10])
            sp.wait_ge(sem("tab_cleared"), 2)
            for l in range(LAYERS):
                sp.dma_start(tabd[l].rearrange("(p b) w -> p b w", p=P), TAB[:, :, :]).then_inc(sem("tab_init"), 16)
            for l in range(LAYERS):
                pl = plans[l]
                if l:
                    ready(sp, l - 1, ("ct", plans[l - 1].t_out - 1, 1))
                load_weights([g for g in loads[0 if l else 10:] if g[0] == l and g[1] != "out"])
                sp.wait_ge(sem("mod_used"), len(mods))
                sp.dma_start(WUQ[:, :, :], A["wuq"][l]).then_inc(sem("wu_in"), 16)
                sp.dma_start(WUKV, A["wukv"][l]).then_inc(sem("wu_in"), 16)
                load_weights([g for g in weights if g[:2] == (l, "out")])
                ready(sp, l, ("wo", KC - 1, pl.sq[-1]))
                sp.dma_start(WB[:, 2, :], A["shared"][l]).then_inc(sem("shared_in"), 16)
                for t in range(pl.t_out):
                    for i in range(2):
                        evacuated(sp, l, ("hr", t, i))
                    sp.dma_start(hrows[l][t * P:(t + 1) * P, :], HROW[:, t % 2, :]).then_inc(sem(f"hrow{t % 2}_{l}"), 16)
                sp.wait_ge(sem(f"meta{l}"), 2)
                nit = sp.value_load(meta[0:1, 0:1], min_val=2, max_val=34)
                for b in range(SLOTS):
                    if b == (2 if pl.t_out == 6 else 1):
                        sp.wait_ge(sem(f"rows_out{l}"), 16 * pl.t_out * TOPK)
                        sp.dma_start(TAB[:, :, :], tabd[l].rearrange("(p b) w -> p b w", p=P)).then_inc(sem("tab_in"), 16)
                        sp.wait_ge(sem(f"gath0_{l}"), 16)
                    if b == 2:
                        ready(sp, l, ("sd", KC - 1, pl.sq[-1]))
                        if l + 1 < LAYERS:
                            load_parameters(l + 1)
                    load_expert(l, b, sp.value_load(eids[0:1, b:b + 1], min_val=0, max_val=EXPERTS - 1))
                with sp.Fori(0, nit - 1) as i:
                    for b in range(SLOTS):
                        e = sp.value_load(eids[0:1, bass.ds(i * SLOTS + (SLOTS + b), 1)], min_val=0, max_val=EXPERTS - 1)
                        sp.wait_ge(sem(f"down{l}"), i * SLOTS + (b + 1))
                        sp.sem_inc(sem("passed"), 1)
                        load_expert(l, b, e)
                sp.wait_ge(sem(f"down{l}"), nit * SLOTS)
                sp.sem_inc(sem("passed"), 1)
                for b in range(SLOTS):
                    sp.wait_ge(sem(f"scat{b}_{l}"), nit * 16 + 16)
                    sp.sem_inc(sem("passed"), 1)
                for t in range(pl.t_out):
                    if t >= 3:
                        ready(sp, l, ("ct", t - 3, 1))
                    for i in range(2):
                        half = slice(i * 512, (i + 1) * 512)
                        sp.dma_start(Y6[:, t % 3, :, half], y6d[l].rearrange("(k t p) d -> t p k d", k=TOPK, p=P)[t][:, :, half]
                                     ).then_inc(sem(f"y6in{t % 3}{i}_{l}"), 16)
            pl, l = plans[-1], LAYERS - 1
            for t in range(pl.t_out):
                sp.wait_ge(sem(f"norm_used{l}"), pl.norm[("nf", t)] + 1)
                sp.dma_start(out[:, :, t * P:(t + 1) * P], H[:, :, t * P:(t + 1) * P]).then_inc(sem("out_done"), 16)
            sp.wait_ge(sem("out_done"), 16 * pl.t_out)

        @block.tensor
        def _(pe):
            mm = nc.tensor.matmul
            pe.wait_ge(sem("silc_ready"), 1)
            for l in range(LAYERS):
                pl = plans[l]
                done = sem(f"pe_jobs{l}")
                first = [0]

                def start_job(key):
                    old = pl.bank_before[key]
                    if old is not None and pl.number[old] >= first[0]:
                        evacuated(pe, l, old)

                def all_evacuated(n):
                    for e in "AD":
                        pe.wait_ge(sem(f"evac{e}{l}"), sum(x == e for _, x in pl.jobs[:n]))
                    first[0] = n

                def group(*g):
                    n = weights.index((l,) + g)
                    pe.wait_ge(sem(f"ring{n % 2}"), 16 * (n // 2 + 1))
                    return RING[:, n % 2, :, :].rearrange("p a (k c) -> p a k c", k=KC)

                def sum_squares(key, mat, n):
                    start_job(key)
                    i0, cnt = pl.square[key]
                    for i in range(cnt):
                        pe.wait_ge(sem(f"sq_ready{l}"), i0 + i + 1)
                        mm(job(l, key, n), c(mat), SQB[:, (i0 + i) % 3, 0:n], start=i == 0, stop=i == cnt - 1
                           ).then_inc(sem(f"sq_used{l}"), 1)

                def product(key, parts, pairs, n):
                    start_job(key)
                    for i, (a, b) in enumerate(pairs):
                        last = mm(job(l, key, n, parts), a, b, start=i == 0, stop=i == len(pairs) - 1)
                    last.then_inc(done, 1)

                if l:
                    for i in range(2):
                        evacuated(pe, l - 1, ("ct", plans[l - 1].t_out - 1, i))
                def z(key, blk, s):
                    a, n = SEG[s]
                    product(key, P, [(blk[:, k, :], H[:, k, a:a + n]) for k in range(KC)], n)

                for st in pl.steps:
                    kind = st[0]
                    if kind == "mod":
                        _, lm, r, k = st
                        n = mods.index((l,) + st)
                        pe.wait_ge(sem(f"mod{n % 3}"), 16 * (n // 3 + 1))
                        m = MODW[n % 3]
                        if k == 0:
                            start_job(("md", lm, r))
                        for q in range(4):
                            last = mm(psum[32 * q:32 * q + 2, 7, :], silc[:, k, :], m[:, q, :], start=k == 0, stop=k == KC - 1)
                        last.then_inc(sem("mod_used"), 1)
                    elif kind == "mt":
                        evacuated(pe, l, ("md",) + st[1:])
                        start_job(st)
                        for q in range(4):
                            last = nc.tensor.transpose(job(l, st)[:, q * P:(q + 1) * P], MROW[:, q * P:(q + 1) * P], ident)
                        last.then_inc(done, 1)
                    elif kind == "n1":
                        if st == ("n1", 0) and l == 0:
                            pe.wait_ge(sem("con_in"), 16)
                        sum_squares(st, "inv1024", SEG[st[1]][1])
                    elif kind == "rot":
                        evacuated(pe, l, ("r" + st[1], 0))
                        product(st, P, [(c("perm"), (RQ if st[1] == "q" else RK)[:, 0:LAT])], LAT)
                    elif kind == "cm":
                        a, n = SEG[st[1]]
                        pe.wait_ge(sem(f"conv_done{l}"), 2 * (pl.sq.index(st[1]) + 1))
                        product(st, P, [(c("inv256"), CAT[:, b, a:a + n]) for b in range(2)], n)
                    elif kind == "cv":
                        sum_squares(st, "inv256", SEG[st[1]][1])
                    elif kind == "in":
                        w = group(*st)
                        if st[1] == 0:
                            pe.wait_ge(sem(f"h_ready{l}"), KC)
                    elif kind in ("g", "a"):
                        if st == ("g", 0, 1):
                            pe.wait_ge(sem(f"h_ready{l}"), 2 * KC)
                        z(st, w[:, 1 if kind == "g" else 0], st[2])
                    elif kind in ("rq", "rk"):
                        if st == ("rk", 1):
                            pe.wait_ge(sem(f"h_ready{l}"), 2 * KC)
                        z(st, w[:, 0 if kind == "rq" else 1], st[1])
                    elif kind in ("rg", "cq"):
                        z(st, w[:, st[1]], st[2])
                    elif kind == "ckv":
                        z(st, w[:, 0], st[1])
                    elif kind == "kr":
                        a, n = SEG[st[1]]
                        start_job(st)
                        for k in range(KC):
                            q = ROPE * (k % 4)
                            last = mm(psum[q:q + ROPE, pl.bank[st], 0:n], w[:, 1, k, 0:ROPE], H[:, k, a:a + n],
                                      start=k < 4, stop=k >= 4)
                        last.then_inc(done, 1)
                    elif kind == "rv":
                        t = st[1]
                        start_job(st)
                        for a in range(2):
                            for k in range(KC):
                                last = mm(job(l, st, 256)[:, a * P:(a + 1) * P], H[:, k, t * P:(t + 1) * P],
                                          w[:, a, k, :], start=k == 0, stop=k == KC - 1)
                        last.then_inc(done, 1)
                for s in (0, 1):
                    a, n = SEG[s]
                    evacuated(pe, l, ("kr", s))
                    product(("kf", s), ROPE, [(c("fold4"), CAT[:, 7, a:a + n])], n)
                evacuated(pe, l, ("kf", 0))
                product(("rot", "kr"), ROPE, [(c("perm", ROPE)[:, 0:ROPE], CAT[0:ROPE, 7, 0:LAT])], LAT)
                for s in pl.sq:
                    sum_squares(("cqn", s), "inv256", SEG[s][1])
                for s in (0, 1):
                    sum_squares(("ckvn", s), "inv128", SEG[s][1])

                all_evacuated(pl.before_retention)
                units = ret_units(l)
                pe.wait_ge(sem(f"rope{l}"), 2)
                pe.wait_ge(sem(f"q_masked{l}"), HEADS_R)

                def ret_scores(u):
                    s, h, kt = units[u]
                    a, n = SEG[s]
                    if u >= 4:
                        pe.wait_ge(sem(f"ret_p{l}"), u - 3)
                    mm(psum[:, u % 4, 0:n], RK[:, kt * P:(kt + 1) * P], QM[:, h, a:a + n],
                       start=True, stop=True).then_inc(sem(f"ret_s{l}"), 1)

                ret_scores(0)
                ret_scores(1)
                for pair in range(0, len(units), 2):
                    if pair + 2 < len(units):
                        ret_scores(pair + 2)
                        ret_scores(pair + 3)
                    pe.wait_ge(sem(f"ret_p{l}"), pair + 2)
                    for u in (pair, pair + 1):
                        s, h, kt = units[u]
                        kts = [x[2] for x in units if x[:2] == (s, h)]
                        half = 64 * (h % 2)
                        mm(psum[half:half + 64, 4 + 2 * s + h // 2, 0:SEG[s][1]], RV[:, kt, h * DV_R:(h + 1) * DV_R],
                           PB[:, u % 4, 0:SEG[s][1]], start=kt == kts[0], stop=kt == kts[-1]).then_inc(sem(f"ret_av{l}"), 1)
                for i in range(2 * len(pl.sq)):
                    pe.wait_ge(sem(f"ret_y{l}"), i + 1)
                for b in range(2):
                    for s in pl.sq:
                        a, n = SEG[s]
                        product(("gm", b, s), P, [(c("headavg"), H[:, b, a:a + n])], n)
                pe.wait_ge(sem("wu_in"), 32 * (l + 1))
                pe.wait_ge(sem(f"norm_used{l}"), pl.norm[("ckvn", 1)] + 1)
                for s in pl.sq:
                    a, n = SEG[s]
                    for i in range(4):
                        product(("qn", i, s), P, [(WUQ[:, k, i * P:(i + 1) * P], CAT[:, 4 + k, a:a + n]) for k in range(2)], n)
                        if s == 0 and i < len(pl.halves):
                            x = pl.halves[i]
                            sum_squares(("gv",) + x, "headavg", SEG[x[1]][1])
                    for r in range(2):
                        product(("qr", r, s), P, [(WUQ[:, k, 512 + r * P:512 + (r + 1) * P], CAT[:, 4 + k, a:a + n])
                                                  for k in range(2)], n)
                    if s == 0:
                        for r in range(2):
                            evacuated(pe, l, ("qr", r, 0))
                            product(("rot2", r), P, [(c("perm"), SQR[:, r, 0:LAT])], LAT)
                for t in range(6):
                    product(("vm", t), P, [(CAT[:, 6, t * P:(t + 1) * P], WUKV[:, 512:1024])], 512)
                for s in (0, 1):
                    a, n = SEG[s]
                    for i in range(4):
                        product(("kn", i, s), P, [(WUKV[:, i * P:(i + 1) * P], CAT[:, 6, a:a + n])], n)

                all_evacuated(pl.before_attention)
                pe.wait_ge(sem(f"qk_ready{l}"), 2)
                units = attn_units(l)
                flat = psum[:, 0:4, :].rearrange("p (u b) n -> p u (b n)", u=2)

                def scores(u):
                    qt, h = units[u]
                    if u >= 2:
                        pe.wait_ge(sem(f"at_p{l}"), u - 1)
                    for i, (a, n) in enumerate(SEG if qt < 4 else SEG[1:]):
                        last = mm(flat[:, u % 2, i * LAT:i * LAT + n], QALL[0:QK, h, qt * P:(qt + 1) * P],
                                  KALL[0:QK, h, a:a + n], start=True, stop=True)
                    last.then_inc(sem(f"at_s{l}"), 1)

                scores(0)
                scores(1)
                for u, (qt, h) in enumerate(units):
                    kts = range(6) if qt < 4 else range(4, 6)
                    pe.wait_ge(sem(f"at_p{l}"), u + 1)
                    if u >= 1:
                        pe.wait_ge(sem(f"at_ta{l}"), u)
                        pe.wait_ge(sem(f"at_tb{l}"), u)
                    for i, kt in enumerate(kts):
                        bk, at = (4 + i // 4, i % 4) if qt < 4 else (4 + i, 0)
                        last = nc.tensor.transpose(psum[:, bk, at * P:(at + 1) * P],
                                                   PR[:, u % 2, i * P:(i + 1) * P], ident)
                    last.then_inc(sem(f"at_t{l}"), 1)
                    if u + 2 < len(units):
                        scores(u + 2)
                    pe.wait_ge(sem(f"at_ta{l}"), u + 1)
                    pe.wait_ge(sem(f"at_tb{l}"), u + 1)
                    if h == 0 and qt >= 1:
                        pe.wait_ge(sem(f"at_o{l}"), qt)
                    for i, kt in enumerate(kts):
                        last = mm(psum[:, 6, h * DV:(h + 1) * DV], PT[:, u % 2, i * P:(i + 1) * P],
                                  VM[:, kt, h * DV:(h + 1) * DV], start=i == 0, stop=i == len(kts) - 1)
                    last.then_inc(sem(f"at_av{l}"), 1)
                    if h == HEADS - 1:
                        pe.wait_ge(sem(f"at_o{l}"), qt + 1)
                        if qt >= 1:
                            pe.wait_ge(sem(f"at_cat{l}"), qt)
                        for i in range(4):
                            last = nc.tensor.transpose(psum[:, 7, i * P:(i + 1) * P], OB[:, qt % 2, i * P:(i + 1) * P], ident)
                        last.then_inc(sem(f"at_ot{l}"), 1)
                pe.wait_ge(sem(f"at_cat{l}"), pl.t_out)
                pe.wait_ge(sem(f"conv_out{l}"), 2 * len(pl.sq))
                pe.wait_ge(sem(f"norm_used{l}"), pl.norm[("gv", 1, pl.sq[-1])] + 1)
                for m in range(KC):
                    if m % 2 == 0:
                        w = group("out", m // 2)
                    for s in pl.sq:
                        a, n = SEG[s]
                        product(("wo", m, s), P, [(w[:, m % 2, k, :], CAT[:, k, a:a + n]) for k in range(KC)], n)
                for s in pl.sq:
                    sum_squares(("n2", s), "inv1024", SEG[s][1])
                rw = pr(l, "router_w").rearrange("p (k e) -> p k e", k=KC)
                for i, (s, a, n) in enumerate(parts(pl.sq)):
                    at = a - SEG[s][0]
                    pe.wait_ge(sem(f"h_ready{l}"), KC * (3 + i))
                    if at == 0:
                        start_job(("rl", s))
                    for k in range(KC):
                        half = EXPERTS * (k % 2)
                        last = mm(psum[half:half + EXPERTS, pl.bank[("rl", s)], at:at + n], rw[:, k, :], H[:, k, a:a + n],
                                  start=k < 2, stop=k >= KC - 2)
                    if a + n == SEG[s][0] + SEG[s][1]:
                        last.then_inc(done, 1)
                start_job("router")
                for t in range(pl.t_out):
                    evacuated(pe, l, ("rl", t // 4))
                    last = mm(job(l, "router")[:, t * EXPERTS:(t + 1) * EXPERTS], LOGIT[:, t * P:(t + 1) * P], c("fold"),
                              start=True, stop=True)
                last.then_inc(done, 1)
                pe.wait_ge(sem("shared_in"), 16 * (l + 1))
                wgu = WB[:, 2, 0:4096].rearrange("p (k f) -> p k f", k=KC)
                wdn = WB[:, 2, 4096:WEXP].rearrange("p (f d) -> p f d", f=2)

                def shared_up(key, f, s):
                    a, n = SEG[s]
                    o = f * P + (FE if key == "su" else 0)
                    product((key, f, s), P, [(wgu[:, k, o:o + P], H[:, k, a:a + n]) for k in range(KC)], n)

                def shared_down(s):
                    a, n = SEG[s]
                    for f in range(2):
                        evacuated(pe, l, ("su", f, s))
                    for m in range(KC):
                        product(("sd", m, s), P, [(wdn[:, f, m * P:(m + 1) * P], ASH[:, f, a:a + n]) for f in range(2)], n)

                shared_up("sg", 0, 0)
                shared_up("su", 0, 0)
                T = pl.t_out
                pe.wait_ge(sem(f"mask{l}"), 2)
                masks = MSK[:, 0:T, :].rearrange("p t e -> p (t e)")
                product("cum", P, [(c("tri"), masks)], T * EXPERTS)
                product("sum", P, [(c("ones"), masks)], T * EXPERTS)
                product("cnt", EXPERTS, [(MSK[:, t, :], c("ones")[:, 0:1]) for t in range(T)], 1)
                shared_up("sg", 1, 0)
                pe.wait_ge(sem(f"blocks{l}"), 1)
                start_job("start")
                mm(job(l, "start", EXPERTS), ncb[:, :], c("tri", EXPERTS)[:, 0:EXPERTS], start=True, stop=True)
                mm(job(l, "start", 65, EXPERTS)[:, 64:65], c("tri", EXPERTS)[:, 0:EXPERTS], ncb[:, 0:1],
                   start=True, stop=True).then_inc(done, 1)
                pe.wait_ge(sem(f"blocks{l}"), 2)
                product("eid", P, [(c("ones", EXPERTS), endge[:, :])], P)
                shared_up("su", 1, 0)
                for t in range(pl.t_out):
                    for i in range(2):
                        start_job(("hr", t, i))
                        for k in range(4):
                            last = nc.tensor.transpose(job(l, ("hr", t, i))[:, k * P:(k + 1) * P],
                                                       H[:, 4 * i + k, t * P:(t + 1) * P], ident)
                        last.then_inc(done, 1)
                shared_down(0)
                for s in pl.sq[1:]:
                    for f in range(2):
                        for key in ("sg", "su"):
                            shared_up(key, f, s)
                    shared_down(s)

                all_evacuated(pl.before_experts)

                def gather_transposed(b):
                    for k in range(KC):
                        last = nc.tensor.transpose(psum[:, 5 + k // 4, (k % 4) * P:(k % 4 + 1) * P],
                                                   HROW[:, b, k * P:(k + 1) * P], ident)
                    last.then_inc(sem(f"rows_T{l}"), 1)

                pe.wait_ge(sem(f"meta{l}"), 2)
                nit = pe.value_load(meta[0:1, 0:1], min_val=2, max_val=34)
                pe.wait_ge(sem(f"gath0_{l}"), 16)
                gather_transposed(0)
                with pe.Fori(0, nit) as i:
                    for b in range(SLOTS):
                        pe.wait_ge(sem(f"wexp{b}_{l}"), i * 16 + 16)
                        pe.wait_ge(sem(f"ht_a{l}"), i * SLOTS + (b + 1))
                        pe.wait_ge(sem(f"ht_d{l}"), i * SLOTS + (b + 1))
                        pe.sem_inc(sem("passed"), 1)
                        for o in range(4):
                            for k in range(KC):
                                last = mm(psum[:, b, o * P:(o + 1) * P], WB[:, b, k * 512 + o * P:k * 512 + (o + 1) * P],
                                          HT[:, b, k, :], start=k == 0, stop=k == KC - 1)
                        last.then_inc(sem(f"gate_up{l}"), 1)
                        nb = (b + 1) % SLOTS
                        pe.wait_ge(sem(f"gath{nb}_{l}"), i * 16 + (16 if nb else 32))
                        pe.sem_inc(sem("passed"), 1)
                        gather_transposed(nb)
                        pe.wait_ge(sem(f"hid{l}"), i * SLOTS + (b + 1))
                        pe.wait_ge(sem(f"y_a{l}"), i * SLOTS + (b + 1))
                        pe.wait_ge(sem(f"y_d{l}"), i * SLOTS + (b + 1))
                        pe.sem_inc(sem("passed"), 1)
                        for j in range(2):
                            for f in range(2):
                                last = mm(psum[:, 3 + j, :], AT[:, b, f, :],
                                          WB[:, b, 4096 + f * D + j * 512:4096 + f * D + (j + 1) * 512], start=f == 0, stop=f == 1)
                        last.then_inc(sem(f"down{l}"), 1)
                pe.wait_ge(sem(f"y_a{l}"), nit * SLOTS + 1)
                pe.wait_ge(sem(f"y_d{l}"), nit * SLOTS + 1)
                pe.wait_ge(sem(f"ht_a{l}"), nit * SLOTS + 1)
                pe.wait_ge(sem(f"ht_d{l}"), nit * SLOTS + 1)
                pe.sem_inc(sem("passed"), 1)
                for t in range(pl.t_out):
                    for i in range(2):
                        pe.wait_ge(sem(f"ysum{l}"), 2 * t + i + 1)
                        start_job(("ct", t, i))
                        for k in range(4):
                            m = 4 * i + k
                            for y in range(3):
                                last = mm(job(l, ("ct", t, i))[:, k * P:(k + 1) * P], Y6[:, t % 3, y, m * P:(m + 1) * P], ident,
                                          start=y == 0, stop=y == 2)
                        last.then_inc(done, 1)
                    if l == LAYERS - 1:
                        key = ("nf", t)
                        start_job(key)
                        for i in range(2):
                            n = pl.square[key][0] + i
                            pe.wait_ge(sem(f"sq_ready{l}"), n + 1)
                            for k in range(4):
                                last = mm(job(l, key, P), c("inv1024"), SQB[:, n % 3, k * P:(k + 1) * P],
                                          start=i == k == 0, stop=i == 1 and k == 3)
                            last.then_inc(sem(f"sq_used{l}"), 1)

        @block.scalar
        def _(act):
            f = nc.scalar.activation
            act.wait_ge(sem("cc_in"), 16)
            f(silc[:, :, :], silc[:, :, :], ACT.Silu).then_inc(sem("silc_ready"), 1)
            act.wait_ge(sem("x_in"), 16)
            act.wait_ge(sem("small_set"), 2)

            def prepare(l):
                act.wait_ge(sem("par_in"), 16 * (l + 1))
                act.wait_ge(sem(f"decay_v{l}"), 1)
                f(lg[:, 2, :], lg[:, 1, :], ACT.Exp, scale=-1.0).then_inc(sem(f"decay_a{l}"), 1)
                act.wait_ge(sem(f"decay_v{l}"), 2)
                f(lg[:, 4, :], lg[:, 3, :], ACT.Ln).then_inc(sem(f"decay_a{l}"), 1)

            for l in range(LAYERS):
                pl, modT = plans[l], modTs[l]
                evacA = sem(f"evacA{l}")

                def squares(key, tiles, n, before=None):
                    i0, cnt = pl.square[key]
                    for i in range(cnt):
                        if before is not None:
                            before(i)
                        if i0 + i >= 3:
                            act.wait_ge(sem(f"sq_used{l}"), i0 + i - 2)
                        f(SQB[:, (i0 + i) % 3, 0:n], tiles[i], ACT.Square).then_inc(sem(f"sq_ready{l}"), 1)

                def root(key, n):
                    i = pl.norm[key]
                    ready(act, l, key)
                    if i >= 4:
                        act.wait_ge(sem(f"norm_used{l}"), i - 3)
                    f(RSB[:, i % 4, 0:n], job(l, key, n), ACT.Sqrt, bias=epsb[:, 0:1]).then_inc(evacA, 1)

                def shift(s, part, count, a, n):
                    for k in range(KC):
                        act.wait_ge(sem(f"scaled{l}"), count + k + 1)
                        f(H[:, k, a:a + n], H[:, k, a:a + n], ACT.Identity, bias=modT[:, part * KC + k, s:s + 1]
                          ).then_inc(sem(f"h_ready{l}"), 1)

                def strip(h):
                    fw, bw, b1, b2 = (lg[:, r, q:q + 1] for r, q in ((8, h), (9, 4 + h), (10, h), (11, 4 + h)))
                    act.wait_ge(sem(f"decay_v{l}"), 5 + 2 * h)
                    f(EX[:, 0, :], DPOS, ACT.Exp, scale=fw)
                    f(EX[:, 1, :], DNEG, ACT.Exp, scale=bw).then_inc(sem(f"decay_a{l}"), 1)
                    act.wait_ge(sem(f"decay_v{l}"), 6 + 2 * h)
                    f(EX[:, 0, 0:STRIP_B], DTAB[:, 256:896], ACT.Exp, scale=fw, bias=b1)
                    f(EX[:, 1, 0:STRIP_B], DTAB[:, 256:896], ACT.Exp, scale=bw, bias=b2).then_inc(sem(f"decay_a{l}"), 1)

                for st in pl.steps:
                    kind = st[0]
                    if kind in ("mod", "in", "a", "rot", "cm"):
                        continue
                    if kind == "cv":
                        a, n = SEG[st[1]]
                        evacuated(act, l, ("cm", st[1]))
                        squares(st, [CAT[:, b, a:a + n] for b in range(2)], n)
                        root(st, n)
                        continue
                    if kind == "n1":
                        a, n = SEG[st[1]]
                        if l:
                            evacuated(act, l - 1, ("ct", (a + n) // P - 1, 1))
                        squares(st, [X[:, k, a:a + n] for k in range(KC)], n)
                        root(st, n)
                        continue
                    if kind == "shift":
                        act.wait_ge(sem(f"A1_ready{l}"), 1)
                        for s in (0, 1):
                            shift(s, 0, KC * s, *SEG[s])
                        if l == 0:
                            prepare(0)
                        continue
                    ready(act, l, st)
                    if kind == "md":
                        for q in range(4):
                            last = f(MROW[32 * q:32 * q + 2, :], psum[32 * q:32 * q + 2, 7, :], ACT.Copy)
                        last.then_inc(evacA, 1)
                        continue
                    if kind == "mt":
                        _, lm, r = st
                        for q in range(4):
                            last = f(modTs[lm][:, 16 * r + 4 * q:16 * r + 4 * q + 4, :],
                                     job(l, st).rearrange("p (c x) -> p c x", c=4)[:, :, 32 * q:32 * q + 2], ACT.Copy)
                        last.then_inc(evacA, 1)
                        evacuated(act, l, st)
                        act.sem_inc(sem(f"mod_rounds{lm}"), 1)
                        continue
                    s = st[-1]
                    a, n = SEG[s] if kind != "rv" else (0, 256)
                    src = job(l, st, n)
                    if kind == "g":
                        op = f(CAT[:, 2 + st[1], a:a + n], src, ACT.Sigmoid)
                    elif kind == "rq":
                        op = f(RQ[:, a:a + n], src, ACT.Copy)
                    elif kind == "rk":
                        op = f(RK[:, a:a + n], src, ACT.Copy, scale=DK_R ** -0.5)
                    elif kind == "rv":
                        op = f(RV[:, s, :], src, ACT.Copy)
                    elif kind == "rg":
                        evacuated(act, l, ("a", st[1], s))
                        op = f(CAT[:, 2 + st[1], a:a + n], src, ACT.Silu)
                    elif kind == "cq":
                        act.wait_ge(sem(f"decay_v{l}"), 5 + 2 * HEADS_R)
                        op = f(CAT[:, 4 + st[1], a:a + n], src, ACT.Copy)
                    elif kind == "ckv":
                        op = f(CAT[:, 6, a:a + n], src, ACT.Copy)
                    elif kind == "kr":
                        op = f(CAT[:, 7, a:a + n], src, ACT.Copy)
                    op.then_inc(evacA, 1)
                    if kind == "g" and s == pl.sq[-1]:
                        for h in range(HEADS_R)[st[1]:1 + st[1] * HEADS_R]:
                            strip(h)
                for s in (0, 1):
                    a, n = SEG[s]
                    ready(act, l, ("kf", s))
                    f(CAT[0:ROPE, 7, a:a + n], job(l, ("kf", s), n, ROPE), ACT.Copy).then_inc(evacA, 1)
                for s in pl.sq:
                    a, n = SEG[s]
                    evacuated(act, l, ("cq", 1, s))
                    squares(("cqn", s), [CAT[:, 4 + b, a:a + n] for b in range(2)], n)
                    root(("cqn", s), n)
                evacuated(act, l, ("ckv", 1))
                for s in (0, 1):
                    a, n = SEG[s]
                    squares(("ckvn", s), [CAT[:, 6, a:a + n]], n)
                    root(("ckvn", s), n)
                for s in pl.sq:
                    a, n = SEG[s]
                    act.wait_ge(sem(f"norm_used{l}"), pl.norm[("cv", s)] + 1)
                    for b in range(2):
                        f(CAT[:, b, a:a + n], CAT[:, b, a:a + n], ACT.Silu, scale=pr(l, "ln_w", b), bias=pr(l, "ln_b", b)
                          ).then_inc(sem(f"conv_out{l}"), 1)
                units = ret_units(l)
                for s in pl.sq:
                    a, n = SEG[s]
                    for b in range(2):
                        act.wait_ge(sem(f"ret_av{l}"), 1 + max(u for u, x in enumerate(units) if x[0] == s and x[1] == 2 * b + 1))
                        f(H[:, b, a:a + n], psum[:, 4 + 2 * s + b, 0:n], ACT.Copy).then_inc(sem(f"ret_y{l}"), 1)
                for s in pl.sq:
                    a, n = SEG[s]
                    for i in range(4):
                        norm = s == 0 and i < len(pl.halves)
                        if norm:
                            b, q = pl.halves[i]
                            at, w = SEG[q]
                            evacuated(act, l, ("gm", b, q))
                            squares(("gv", b, q), [H[:, b, at:at + w]], w)
                        ready(act, l, ("qn", i, s))
                        f(QALL[0:64, 2 * i, a:a + n], job(l, ("qn", i, s), n)[0:64], ACT.Copy)
                        f(QALL[0:64, 2 * i + 1, a:a + n], job(l, ("qn", i, s), n)[64:128], ACT.Copy).then_inc(evacA, 1)
                        if norm:
                            root(("gv", b, q), w)
                    for r in range(2):
                        ready(act, l, ("qr", r, s))
                        if s == 0:
                            f(SQR[:, r, 0:n], job(l, ("qr", r, s), n), ACT.Copy).then_inc(evacA, 1)
                        else:
                            for j in range(4):
                                last = f(QALL[64:96, 4 * r + j, a:a + n], job(l, ("qr", r, s), n)[32 * j:32 * j + 32], ACT.Copy)
                            last.then_inc(evacA, 1)
                for t in range(6):
                    ready(act, l, ("vm", t))
                    f(VM[:, t, :], job(l, ("vm", t)), ACT.Copy).then_inc(evacA, 1)
                act.wait_ge(sem(f"norm_used{l}"), pl.norm[("gv", 1, pl.sq[-1])] + 1)
                for s in (0, 1):
                    a, n = SEG[s]
                    for i in (0, 2):
                        ready(act, l, ("kn", i, s))
                        f(KALL[0:64, 2 * i, a:a + n], job(l, ("kn", i, s), n)[0:64], ACT.Copy)
                        f(KALL[0:64, 2 * i + 1, a:a + n], job(l, ("kn", i, s), n)[64:128], ACT.Copy).then_inc(evacA, 1)

                units = attn_units(l)
                flat = psum[:, 0:4, :].rearrange("p (u b) n -> p u (b n)", u=2)

                def exps(u):
                    qt, h = units[u]
                    n = TOK if qt < 4 else CTX
                    act.wait_ge(sem(f"at_m{l}"), u + 1)
                    if u >= 2:
                        act.wait_ge(sem(f"at_t{l}"), u - 1)
                    f(PR[:, u % 2, 0:n], flat[:, u % 2, 0:n], ACT.Exp, bias=nm[:, u % 4:u % 4 + 1], scale=QK ** -0.5,
                      accum_out=rsum[:, qt % 2, h:h + 1]).then_inc(sem(f"at_p{l}"), 1)

                def outputs(qt):
                    act.wait_ge(sem(f"at_ot{l}"), qt + 1)
                    f(CAT[:, 4:8, qt * P:(qt + 1) * P], psum[:, 7, :].rearrange("p (a b) -> p a b", a=4), ACT.Copy
                      ).then_inc(sem(f"at_cat{l}"), 1)

                exps(0)
                for u, (qt, h) in enumerate(units):
                    if u + 1 < len(units):
                        exps(u + 1)
                    act.wait_ge(sem(f"at_t{l}"), u + 1)
                    if u >= 2:
                        act.wait_ge(sem(f"at_av{l}"), u - 1)
                    src, dst = (psum[:, 5, 0:256], slice(512, 768)) if qt < 4 else (psum[:, 5, 0:128], slice(128, 256))
                    f(PT[:, u % 2, dst], src, ACT.Copy).then_inc(sem(f"at_tb{l}"), 1)
                    if h == 1 and qt >= 1:
                        outputs(qt - 1)
                outputs(pl.t_out - 1)
                for s in pl.sq:
                    a, n = SEG[s]
                    squares(("n2", s), [X[:, k, a:a + n] for k in range(KC)], n, lambda k: evacuated(act, l, ("wo", k, s)))
                    root(("n2", s), n)
                for i, (s, a, n) in enumerate(parts(pl.sq)):
                    shift(s, 3, KC * (2 + i), a, n)
                for s in pl.sq:
                    a, n = SEG[s]
                    ready(act, l, ("rl", s))
                    f(LOGIT[:, a:a + n], job(l, ("rl", s), n), ACT.Copy).then_inc(evacA, 1)
                ready(act, l, "router")
                f(SC[:, 0:pl.t_out, :], job(l, "router", pl.t_out * EXPERTS).rearrange("p (t e) -> p t e", t=pl.t_out),
                  ACT.Sigmoid).then_inc(evacA, 1)
                for i, s in enumerate(pl.sq):
                    n = SEG[s][1]
                    for j in range(2):
                        ready(act, l, ("sg", j, s))
                        if i:
                            evacuated(act, l, ("su", j, pl.sq[i - 1]))
                        f(SGS[:, j, 0:n], job(l, ("sg", j, s), n), ACT.Silu).then_inc(evacA, 1)
                    if s == 0:
                        for t in range(pl.t_out):
                            if t >= 2:
                                act.wait_ge(sem(f"hrow{t % 2}_{l}"), 16 * (t // 2))
                            for q in range(2):
                                ready(act, l, ("hr", t, q))
                                f(HROW[:, t % 2, q * 512:(q + 1) * 512], job(l, ("hr", t, q)), ACT.Copy).then_inc(evacA, 1)

                act.wait_ge(sem(f"meta{l}"), 2)
                nit = act.value_load(meta[0:1, 0:1], min_val=2, max_val=34)
                act.wait_ge(sem(f"rows_T{l}"), 1)
                f(HT[:, 0, 0:4, :], psum[:, 5, :].rearrange("p (k c) -> p k c", k=4), ACT.Copy).then_inc(sem(f"ht_a{l}"), 1)
                act.sem_inc(sem(f"y_a{l}"), 1)
                with act.Fori(0, nit) as i:
                    for b in range(SLOTS):
                        nb = (b + 1) % SLOTS
                        act.wait_ge(sem(f"gate_up{l}"), i * SLOTS + (b + 1))
                        f(SG[:, b, :, :], psum[:, b, 0:256].rearrange("p (a c) -> p a c", a=2), ACT.Silu
                          ).then_inc(sem(f"gates{l}"), 1)
                        act.wait_ge(sem(f"rows_T{l}"), i * SLOTS + (b + 2))
                        f(HT[:, nb, 0:4, :], psum[:, 5, :].rearrange("p (k c) -> p k c", k=4), ACT.Copy
                          ).then_inc(sem(f"ht_a{l}"), 1)
                        act.wait_ge(sem(f"down{l}"), i * SLOTS + (b + 1))
                        act.wait_ge(sem(f"scat{b}_{l}"), i * 16 + 16)
                        act.wait_ge(sem(f"six{l}"), i * SLOTS + (b + 1))
                        f(YB[:, b, 0:512], psum[:, 3, :], ACT.Copy, scale=SIX[:, b, 2:3].bitcast(F32)
                          ).then_inc(sem(f"y_a{l}"), 1)
                if l + 1 < LAYERS:
                    prepare(l + 1)
                if l == LAYERS - 1:
                    for t in range(pl.t_out):
                        for i in range(2):
                            evacuated(act, l, ("ct", t, i))
                            n = pl.square[("nf", t)][0] + i
                            act.wait_ge(sem(f"sq_used{l}"), n - 2)
                            f(SQB[:, n % 3, :].rearrange("p (k c) -> p k c", k=4), X[:, 4 * i:4 * i + 4, t * P:(t + 1) * P],
                              ACT.Square).then_inc(sem(f"sq_ready{l}"), 1)
                        root(("nf", t), P)

        @block.vector
        def _(dve):
            V = nc.vector
            link = chain(dve, sem("dve_order"))
            V.memset(epsb[:, :], EPS).then_inc(sem("small_set"), 1)
            V.memset(MROW, 0.0).then_inc(sem("small_set"), 1)
            V.memset(TAB[:, :, 0:2], BIG).then_inc(sem("tab_cleared"), 1)
            V.memset(TAB[:, :, 2:4], 0).then_inc(sem("tab_cleared"), 1)
            dve.wait_ge(sem("con_in"), 16)
            dve.wait_ge(sem("x_in"), 16)
            iota = c("iota64")

            def modulation(l, m0, m1):
                m = modTs[l][:, m0:m1, :].rearrange("p m s -> p (m s)")
                link(V.tensor_tensor(m, m, pr(l, "mod_b")[:, 2 * m0:2 * m1], ALU.add))

            def norm_scale(l, dst, part, w):
                link(V.scalar_tensor_tensor(dst[:, :, :].rearrange("p k s -> p (k s)"),
                                            modTs[l][:, part * KC:(part + 1) * KC, :].rearrange("p k s -> p (k s)"),
                                            1.0, pr(l, w), ALU.add, ALU.mult))

            def prepare(l):
                dve.wait_ge(sem("par_in"), 16 * (l + 1))
                x8 = pr(l, "decay")
                link(V.tensor_scalar(lg[:, 0, :], x8, -1.0, None, ALU.mult))
                V.tensor_tensor(lg[:, 1, :], lg[:, 0, :], x8, ALU.max).then_inc(sem(f"decay_v{l}"), 1)
                dve.wait_ge(sem(f"decay_a{l}"), 1)
                V.tensor_scalar(lg[:, 3, :], lg[:, 2, :], 1.0, None, ALU.add).then_inc(sem(f"decay_v{l}"), 1)
                dve.wait_ge(sem(f"decay_v{l}"), 2)
                link(V.tensor_scalar(lg[:, 5, :], lg[:, 3, :], 1.0, None, ALU.subtract))
                link(V.tensor_scalar(lg[:, 6, :], lg[:, 5, :], 0.0, None, ALU.is_equal))
                link(V.tensor_tensor(lg[:, 5, :], lg[:, 5, :], lg[:, 6, :], ALU.add))
                link(V.reciprocal(lg[:, 7, :], lg[:, 5, :]))
                link(V.tensor_tensor(lg[:, 7, :], lg[:, 7, :], lg[:, 2, :], ALU.mult))
                link(V.tensor_tensor(lg[:, 6, :], lg[:, 6, :], lg[:, 2, :], ALU.mult))
                dve.wait_ge(sem(f"decay_a{l}"), 2)
                link(V.tensor_tensor(lg[:, 7, :], lg[:, 7, :], lg[:, 4, :], ALU.mult))
                link(V.tensor_tensor(lg[:, 7, :], lg[:, 7, :], lg[:, 6, :], ALU.add))
                link(V.scalar_tensor_tensor(lg[:, 8, :], x8, 0.0, lg[:, 7, :], ALU.min, ALU.subtract))
                link(V.tensor_scalar(lg[:, 9, :], lg[:, 8, :], -1.0, None, ALU.mult))
                link(V.tensor_scalar(lg[:, 10, :], lg[:, 8, :], float(CTX), None, ALU.mult))
                V.tensor_scalar(lg[:, 11, :], lg[:, 8, :], float(LAT), None, ALU.mult).then_inc(sem(f"decay_v{l}"), 1)

            def modulate(l):
                dve.wait_ge(sem(f"mod_rounds{l}"), 1 if l == 0 else 3)
                modulation(l, 0, 16 if l == 0 else MOD)
                norm_scale(l, A1, 1, "n1")
                dve.sem_inc(sem(f"A1_ready{l}"), 1)

            for l in range(LAYERS):
                pl, modT = plans[l], modTs[l]
                evacD = sem(f"evacD{l}")
                norm_used = sem(f"norm_used{l}")

                def recip(key, n, at=0):
                    evacuated(dve, l, key)
                    r = RSB[:, pl.norm[key] % 4, at:at + n]
                    link(V.reciprocal(r, r))
                    return r

                def scaled(key, s, A, r=None, part=None):
                    a, n = part or SEG[s]
                    r = recip(key, n, a - SEG[s][0]) if r is None else r
                    for k in range(KC):
                        last = V.scalar_tensor_tensor(H[:, k, a:a + n], X[:, k, a:a + n], A[:, k, s:s + 1], r, ALU.mult, ALU.mult)
                        last.then_inc(sem(f"scaled{l}"), 1)
                    dve.wait_ge(sem(f"scaled{l}"), scaled_at[0] + KC)
                    scaled_at[0] += KC
                    if a + n == SEG[s][0] + SEG[s][1]:
                        dve.sem_inc(norm_used, 1)

                scaled_at = [0]
                link(V.memset(HPAD[:, :, :], 0.0))
                early = [recip(("n1", s), SEG[s][1]) for s in (0, 1)] if l == 0 else [None] * 2
                if l == 0:
                    modulate(0)
                for s in (0, 1):
                    scaled(("n1", s), s, A1, early[s])
                if l == 0:
                    prepare(0)
                dve.wait_ge(sem("dtab_in"), 16 * (l + 1))
                V.tensor_scalar(DPOS, DTAB, 0.0, None, ALU.max).then_inc(sem(f"decay_v{l}"), 1)
                V.tensor_scalar(DNEG, DTAB, 0.0, None, ALU.min).then_inc(sem(f"decay_v{l}"), 1)

                def strip(h):
                    dve.wait_ge(sem(f"decay_a{l}"), 2 * h + 3)
                    link(V.scalar_tensor_tensor(EX[:, 0, :], DTAB, 0.0, EX[:, 0, :], ALU.is_ge, ALU.mult))
                    link(V.scalar_tensor_tensor(EX[:, 1, :], DTAB, 0.0, EX[:, 1, :], ALU.is_le, ALU.mult))
                    V.tensor_tensor(SA[:, h, :], EX[:, 0, :], EX[:, 1, :], ALU.add).then_inc(sem(f"decay_v{l}"), 1)
                    dve.wait_ge(sem(f"decay_a{l}"), 2 * h + 4)
                    V.tensor_tensor(SB[:, h, :], EX[:, 0, 0:STRIP_B], EX[:, 1, 0:STRIP_B], ALU.add).then_inc(sem(f"decay_v{l}"), 1)

                for b in range(2):
                    for s in pl.sq:
                        a, n = SEG[s]
                        ready(dve, l, ("a", b, s))
                        evacuated(dve, l, ("g", b, s))
                        V.tensor_tensor(HPAD[:, b, PADAT[s]:PADAT[s] + n], job(l, ("a", b, s), n), CAT[:, 2 + b, a:a + n], ALU.mult
                                        ).then_inc(evacD, 1)
                    for h in range(HEADS_R)[b:1 + b * HEADS_R]:
                        strip(h)
                evacuated(dve, l, ("a", 1, pl.sq[-1]))
                chains = [(s, b) for s in pl.sq for b in range(2)]
                for k in range(CK):
                    for i, (s, b) in enumerate(chains):
                        a, n = SEG[s]
                        src = HPAD[:, b, PADAT[s] - 15 + k:PADAT[s] - 15 + k + n]
                        dst = CAT[:, b, a:a + n]
                        w = pr(l, "conv_w", b * CK + k)
                        if k == 0:
                            op = V.tensor_scalar(dst, src, w, pr(l, "conv_b", b), ALU.mult, ALU.add)
                        else:
                            dve.wait_ge(sem(f"conv_step{l}"), (k - 1) * len(chains) + i + 1)
                            op = V.scalar_tensor_tensor(dst, src, w, dst, ALU.mult, ALU.add)
                        op.then_inc(sem(f"conv_step{l}" if k < CK - 1 else f"conv_done{l}"), 1)
                def rope(name, x, parts):
                    ready(dve, l, ("rot", name))
                    V.tensor_tensor(TMP[0:parts], job(l, ("rot", name), LAT, parts), c("sin", parts), ALU.mult).then_inc(evacD, 1)
                    link(V.tensor_tensor(x, x, c("cos", parts), ALU.mult))
                    evacuated(dve, l, ("rot", name))
                    V.tensor_tensor(x, x, TMP[0:parts], ALU.add).then_inc(sem(f"rope{l}"), 1)
                    dve.wait_ge(sem(f"rope{l}"), ("q", "k", "kr").index(name) + 1)

                rope("q", RQ[:, 0:LAT], P)
                rope("k", RK[:, 0:LAT], P)
                dve.wait_ge(sem(f"conv_done{l}"), len(chains))
                for s in pl.sq:
                    a, n = SEG[s]
                    ready(dve, l, ("cm", s))
                    for b in range(2):
                        last = V.tensor_tensor(CAT[:, b, a:a + n], CAT[:, b, a:a + n], job(l, ("cm", s), n), ALU.subtract)
                    last.then_inc(evacD, 1)
                for s in pl.sq:
                    a, n = SEG[s]
                    r = recip(("cv", s), n)
                    for b in range(2):
                        last = V.tensor_tensor(CAT[:, b, a:a + n], CAT[:, b, a:a + n], r, ALU.mult)
                    last.then_inc(norm_used, 1)
                if l == 0:
                    dve.wait_ge(sem(f"mod_rounds{l}"), 3)
                    modulation(l, 16, MOD)
                norm_scale(l, A2, 4, "n2")
                ready(dve, l, ("kr", 1))
                w = SEG[pl.sq[-1]][0] + SEG[pl.sq[-1]][1]
                for s in pl.sq:
                    evacuated(dve, l, ("rq", s))
                for h in range(HEADS_R):
                    V.tensor_scalar(QM[:, h, 0:w], RQ[:, 0:w], c("headmask")[:, h:h + 1], None, ALU.mult
                                    ).then_inc(sem(f"q_masked{l}"), 1)
                rope("kr", CAT[0:ROPE, 7, 0:LAT], ROPE)
                latents = [("cqn", s, ((4, "qn", 0), (5, "qn", 1))) for s in pl.sq] + [("ckvn", s, ((6, "kvn", 0),)) for s in (0, 1)]
                for u, (s, h, kt) in enumerate(ret_units(l)):
                    if u % 4 == 3 and latents:
                        key, q, chunks = latents.pop(0)
                        a, n = SEG[q]
                        r = recip((key, q), n)
                        for k, w, i in chunks:
                            last = V.scalar_tensor_tensor(CAT[:, k, a:a + n], CAT[:, k, a:a + n], pr(l, w, i), r, ALU.mult, ALU.mult)
                        last.then_inc(norm_used, 1)
                    n = SEG[s][1]
                    if s == 0 and kt >= 4:
                        m0 = P - P * (kt - 4)
                        strip = SB[:, h, m0:m0 + n]
                    else:
                        m0 = 384 - P * (kt if s == 0 else kt - 4)
                        strip = SA[:, h, m0:m0 + n]
                    dve.wait_ge(sem(f"ret_s{l}"), u + 1)
                    if u >= 4:
                        dve.wait_ge(sem(f"ret_av{l}"), u - 3)
                    V.tensor_tensor(PB[:, u % 4, 0:n], psum[:, u % 4, 0:n], strip, ALU.mult).then_inc(sem(f"ret_p{l}"), 1)
                for b in range(2):
                    for s in pl.sq:
                        a, n = SEG[s]
                        ready(dve, l, ("gm", b, s))
                        V.tensor_tensor(H[:, b, a:a + n], H[:, b, a:a + n], job(l, ("gm", b, s), n), ALU.subtract).then_inc(evacD, 1)
                for b in range(2):
                    for s in pl.sq:
                        a, n = SEG[s]
                        y = H[:, b, a:a + n]
                        r = recip(("gv", b, s), n)
                        link(V.tensor_tensor(y, y, r, ALU.mult))
                        V.scalar_tensor_tensor(CAT[:, 2 + b, a:a + n], y, pr(l, "gn_w", b), CAT[:, 2 + b, a:a + n], ALU.mult, ALU.mult
                                               ).then_inc(norm_used, 1)
                dve.wait_ge(norm_used, pl.norm[("gv", 1, pl.sq[-1])] + 1)
                for r in range(2):
                    ready(dve, l, ("rot2", r))
                    link(V.tensor_tensor(TMP, job(l, ("rot2", r)), c("sin"), ALU.mult))
                    link(V.tensor_tensor(SQR[:, r, :], SQR[:, r, :], c("cos"), ALU.mult))
                    for j in range(4):
                        last = V.tensor_tensor(QALL[64:96, 4 * r + j, 0:LAT], SQR[32 * j:32 * j + 32, r, :],
                                               TMP[32 * j:32 * j + 32], ALU.add)
                    last.then_inc(evacD, 1)
                    evacuated(dve, l, ("rot2", r))
                evacuated(dve, l, ("kf", 1))
                V.tensor_copy(KALL[64:96, 0:2, :], CAT[0:ROPE, 7:8, :].to_broadcast([ROPE, 2, TOK])
                              ).then_inc(sem(f"qk_ready{l}"), 1)
                for s in (0, 1):
                    a, n = SEG[s]
                    for i in (1, 3):
                        ready(dve, l, ("kn", i, s))
                        V.tensor_copy(KALL[0:64, 2 * i, a:a + n], job(l, ("kn", i, s), n)[0:64])
                        V.tensor_copy(KALL[0:64, 2 * i + 1, a:a + n], job(l, ("kn", i, s), n)[64:128]).then_inc(evacD, 1)
                units = attn_units(l)
                flat = psum[:, 0:4, :].rearrange("p (u b) n -> p u (b n)", u=2)

                def maxima(u):
                    n = TOK if units[u][0] < 4 else CTX
                    dve.wait_ge(sem(f"at_s{l}"), u + 1)
                    q = slice(u % 4, u % 4 + 1)
                    link(V.reduce_max(mx[:, q], flat[:, u % 2, 0:n], AX))
                    V.tensor_scalar(nm[:, q], mx[:, q], -QK ** -0.5, None, ALU.mult).then_inc(sem(f"at_m{l}"), 1)

                maxima(0)
                for u, (qt, h) in enumerate(units):
                    if u + 1 < len(units):
                        maxima(u + 1)
                    dve.wait_ge(sem(f"at_t{l}"), u + 1)
                    if u >= 2:
                        dve.wait_ge(sem(f"at_av{l}"), u - 1)
                    n = 512 if qt < 4 else P
                    V.tensor_copy(PT[:, u % 2, 0:n], psum[:, 4, 0:n]).then_inc(sem(f"at_ta{l}"), 1)
                    if h == HEADS - 1:
                        dve.wait_ge(sem(f"at_av{l}"), u + 1)
                        link(V.reciprocal(rinv[:, qt % 2, :], rsum[:, qt % 2, :]))
                        V.tensor_tensor(OB[:, qt % 2, :].rearrange("p (h d) -> p h d", h=HEADS),
                                        psum[:, 6, :].rearrange("p (h d) -> p h d", h=HEADS),
                                        rinv[:, qt % 2, :].unsqueeze(2).to_broadcast([P, HEADS, DV]), ALU.mult
                                        ).then_inc(sem(f"at_o{l}"), 1)
                for m in range(KC):
                    for s in pl.sq:
                        a, n = SEG[s]
                        ready(dve, l, ("wo", m, s))
                        V.scalar_tensor_tensor(X[:, m, a:a + n], job(l, ("wo", m, s), n), modT[:, 2 * KC + m, s:s + 1],
                                               X[:, m, a:a + n], ALU.mult, ALU.add).then_inc(evacD, 1)
                for s in pl.sq:
                    evacuated(dve, l, ("wo", KC - 1, s))
                for s, a, n in parts(pl.sq):
                    scaled(("n2", s), s, A2, part=(a, n))
                dve.wait_ge(sem("pay_in"), 16 * (l + 1))
                evacuated(dve, l, "router")
                def shared_hidden(j, s):
                    a, n = SEG[s]
                    ready(dve, l, ("su", j, s))
                    evacuated(dve, l, ("sg", j, s))
                    V.tensor_tensor(ASH[:, j, a:a + n], job(l, ("su", j, s), n), SGS[:, j, 0:n], ALU.mult).then_inc(evacD, 1)

                T = pl.t_out
                sel = QUO[:, 0:T, :]
                link(V.tensor_tensor(sel, SC[:, 0:T, :], pr(l, "router_b").unsqueeze(1).to_broadcast([P, T, EXPERTS]), ALU.add))
                for t in range(T):
                    last = V.max(rt[:, t, 0, :], sel[:, t, :])
                link(last)
                for t in range(T):
                    last = V.max_index(rtu[:, t, :], rt[:, t, 0, :], sel[:, t, :])
                link(last)
                link(V.tensor_copy(rt[:, 0:T, 1, :], rtu[:, 0:T, :]))
                halves = [slice(0, T // 2), slice(T // 2, T)]

                def one_hot(ts):
                    return OH[:, ts.start * TOPK:ts.stop * TOPK, :]

                def pick(dst, src, ts):
                    n = ts.stop - ts.start
                    prod = PICK[:, 0:n * TOPK, :].rearrange("p (t k) e -> p t k e", k=TOPK)
                    link(V.tensor_tensor(prod, one_hot(ts).rearrange("p (t k) e -> p t k e", k=TOPK),
                                         src[:, ts, :].unsqueeze(2).to_broadcast([P, n, TOPK, EXPERTS]), ALU.mult))
                    link(V.reduce_sum(rt[:, ts, dst, 0:TOPK], prod, AX))

                for ts in halves:
                    n = ts.stop - ts.start
                    oh = one_hot(ts).rearrange("p (t k) e -> p t k e", k=TOPK)
                    link(V.tensor_tensor(oh, iota.unsqueeze(1).unsqueeze(1).to_broadcast([P, n, TOPK, EXPERTS]),
                                         rt[:, ts, 1, 0:TOPK].unsqueeze(3).to_broadcast([P, n, TOPK, EXPERTS]), ALU.is_equal))
                    V.reduce_sum(MSK[:, ts, :], one_hot(ts).rearrange("p (t k) e -> p t e k", k=TOPK), AX
                                 ).then_inc(sem(f"mask{l}"), 1)
                for ts in halves:
                    pick(2, SC, ts)
                link(V.reduce_sum(rt[:, 0:T, 4, 0:1], rt[:, 0:T, 2, 0:TOPK], AX))
                link(V.reciprocal(rt[:, 0:T, 4, 1:2], rt[:, 0:T, 4, 0:1]))
                for t in range(T):
                    last = V.tensor_scalar(PAYF[:, t, :, 2], rt[:, t, 2, 0:TOPK], rt[:, t, 4, 1:2], ROUTED_SCALE,
                                           ALU.mult, ALU.mult)
                link(last)
                shared_hidden(0, 0)
                ready(dve, l, "cum")
                V.tensor_copy(ROWP[:, 0:T, :], job(l, "cum", T * EXPERTS).rearrange("p (t e) -> p t e", t=T)).then_inc(evacD, 1)
                ready(dve, l, "sum")
                V.tensor_copy(SUMS[:, 0:T, :], job(l, "sum", T * EXPERTS).rearrange("p (t e) -> p t e", t=T)).then_inc(evacD, 1)
                ready(dve, l, "cnt")
                V.tensor_copy(col[:, 0:1], job(l, "cnt", 1, EXPERTS)).then_inc(evacD, 1)
                evacuated(dve, l, "cnt")
                for t in range(1, T):
                    link(V.tensor_tensor(SUMS[:, t, :], SUMS[:, t, :], SUMS[:, t - 1, :], ALU.add))
                V.tensor_copy(CNT[:, 0, :], SUMS[:, T - 1, :])
                link(V.tensor_tensor(ROWP[:, 1:T, :], ROWP[:, 1:T, :], SUMS[:, 0:T - 1, :], ALU.add))
                for dst, src in ((CNT[:, 1, :], CNT[:, 0, :]), (col[:, 1:2], col[:, 0:1])):
                    link(V.tensor_scalar(dst, src, 0.0, None, ALU.is_gt))
                    for q in range(1, T):
                        link(V.scalar_tensor_tensor(dst, src, float(P * q), dst, ALU.is_gt, ALU.add))
                V.tensor_copy(ncb[:, :], col[:, 1:2].to_broadcast([EXPERTS, P])).then_inc(sem(f"blocks{l}"), 1)
                link(V.tensor_scalar(QUO[:, 0:T, :], ROWP[:, 0:T, :], float(P), None, ALU.is_ge))
                for q in range(2, T):
                    link(V.scalar_tensor_tensor(QUO[:, 0:T, :], ROWP[:, 0:T, :], float(P * q), QUO[:, 0:T, :], ALU.is_ge, ALU.add))
                ready(dve, l, "start")
                V.tensor_copy(CNT[:, 2, :], job(l, "start", EXPERTS))
                V.tensor_tensor(col[:, 2:3], job(l, "start", 65, EXPERTS)[:, 64:65], col[:, 1:2], ALU.add).then_inc(evacD, 1)
                evacuated(dve, l, "start")
                V.tensor_scalar(endge[:, :], c("iota128", EXPERTS), col[:, 2:3], None, ALU.is_ge).then_inc(sem(f"blocks{l}"), 1)
                link(V.tensor_tensor(CNT[:, 3, :], CNT[:, 1, :], CNT[:, 2, :], ALU.add))
                link(V.tensor_scalar(metaf[0:1, 0:P], c("iota128", 1), float(SLOTS), CNT[0:1, 3, EXPERTS - 1:EXPERTS], ALU.mult, ALU.is_lt))
                link(V.reduce_sum(metaf[0:1, P:P + 1], metaf[0:1, 0:P], AX))
                V.tensor_copy(meta[0:1, 0:1], metaf[0:1, P:P + 1]).then_inc(sem(f"meta{l}"), 1)
                link(V.scalar_tensor_tensor(ROWP[:, 0:T, :], ROWP[:, 0:T, :], float(BLOCKS),
                                            CNT[:, 2:3, :].to_broadcast([P, T, EXPERTS]), ALU.mult, ALU.add))
                link(V.scalar_tensor_tensor(ROWP[:, 0:T, :], QUO[:, 0:T, :], float(1 - BLOCKS * P), ROWP[:, 0:T, :],
                                            ALU.mult, ALU.add))
                ready(dve, l, "eid")
                V.tensor_scalar(eids[0:1, :], job(l, "eid", P, 1), float(EXPERTS - 1), None, ALU.min).then_inc(evacD, 1)
                evacuated(dve, l, "eid")
                dve.sem_inc(sem(f"meta{l}"), 1)
                for t in range(T):
                    if t == 2:
                        shared_hidden(1, 0)
                    pick(3, ROWP, slice(t, t + 1))
                    V.tensor_copy(dsti[:, t, 0:TOPK], rt[:, t, 3, 0:TOPK]).then_inc(sem(f"dest{l}"), 1)
                for s in pl.sq:
                    a, n = SEG[s]
                    if s:
                        for j in range(2):
                            shared_hidden(j, s)
                    for m in range(KC):
                        ready(dve, l, ("sd", m, s))
                        V.scalar_tensor_tensor(X[:, m, a:a + n], job(l, ("sd", m, s), n), modT[:, 5 * KC + m, s:s + 1],
                                               X[:, m, a:a + n], ALU.mult, ALU.add).then_inc(evacD, 1)
                nit = dve.value_load(meta[0:1, 0:1], min_val=2, max_val=34)
                dve.wait_ge(sem(f"rows_T{l}"), 1)
                V.tensor_copy(HT[:, 0, 4:8, :], psum[:, 6, :].rearrange("p (k c) -> p k c", k=4)).then_inc(sem(f"ht_d{l}"), 1)
                dve.sem_inc(sem(f"y_d{l}"), 1)
                with dve.Fori(0, nit) as i:
                    for b in range(SLOTS):
                        nb = (b + 1) % SLOTS
                        dve.wait_ge(sem(f"gates{l}"), i * SLOTS + (b + 1))
                        V.tensor_tensor(AT[:, b, :, :], psum[:, b, 256:512].rearrange("p (a c) -> p a c", a=2), SG[:, b, :, :],
                                        ALU.mult).then_inc(sem(f"hid{l}"), 1)
                        dve.wait_ge(sem(f"rows_T{l}"), i * SLOTS + (b + 2))
                        V.tensor_copy(HT[:, nb, 4:8, :], psum[:, 6, :].rearrange("p (k c) -> p k c", k=4)
                                      ).then_inc(sem(f"ht_d{l}"), 1)
                        dve.wait_ge(sem(f"down{l}"), i * SLOTS + (b + 1))
                        dve.wait_ge(sem(f"scat{b}_{l}"), i * 16 + 16)
                        dve.wait_ge(sem(f"six{l}"), i * SLOTS + (b + 1))
                        V.tensor_scalar(YB[:, b, 512:1024], psum[:, 4, :], SIX[:, b, 2:3].bitcast(F32), None, ALU.mult
                                        ).then_inc(sem(f"y_d{l}"), 1)
                if l + 1 < LAYERS:
                    prepare(l + 1)
                    modulate(l + 1)
                dve.wait_ge(sem(f"gathers_done{l}"), 1)

                def last_norm(t):
                    r = recip(("nf", t), P)
                    for k in range(KC):
                        last = V.scalar_tensor_tensor(H[:, k, t * P:(t + 1) * P], X[:, k, t * P:(t + 1) * P], pr(l, "final", k), r,
                                                      ALU.mult, ALU.mult)
                    last.then_inc(norm_used, 1)

                def gated(t):
                    for i in range(2):
                        ready(dve, l, ("ct", t, i))
                        for k in range(4):
                            m = 4 * i + k
                            last = V.scalar_tensor_tensor(X[:, m, t * P:(t + 1) * P], job(l, ("ct", t, i))[:, k * P:(k + 1) * P],
                                                          modT[:, 5 * KC + m, t // 4:t // 4 + 1], X[:, m, t * P:(t + 1) * P],
                                                          ALU.mult, ALU.add)
                        last.then_inc(evacD, 1)

                for t in range(T):
                    for i in range(2):
                        dve.wait_ge(sem(f"y6in{t % 3}{i}_{l}"), 16 * (t // 3 + 1))
                        y = Y6[:, t % 3, :, i * 512:(i + 1) * 512]
                        V.tensor_tensor(y[:, 0:3, :], y[:, 0:3, :], y[:, 3:6, :], ALU.add).then_inc(sem(f"ysum{l}"), 1)
                    if l < LAYERS - 1:
                        if t:
                            gated(t - 1)
                        if t == T - 1:
                            gated(t)
                    else:
                        if t:
                            last_norm(t - 1)
                        gated(t)
                evacuated(dve, l, ("ct", T - 1, 1))
                if l == LAYERS - 1:
                    last_norm(T - 1)

        @block.gpsimd
        def _(pool):
            g = nc.gpsimd

            def offsets(ap):
                return bass.IndirectOffsetOnAxis(ap=ap.bitcast(U32), axis=0)

            for l in range(LAYERS):
                pl = plans[l]
                T = pl.t_out
                pool.wait_ge(sem(f"rope{l}"), 3)
                evacuated(pool, l, ("kf", 1))
                pool.wait_ge(sem(f"ret_s{l}"), len(ret_units(l)))
                g.tensor_copy(KALL[64:96, 2:HEADS, :], CAT[0:ROPE, 7:8, :].to_broadcast([ROPE, HEADS - 2, TOK])
                              ).then_inc(sem(f"qk_ready{l}"), 1)
                pool.wait_ge(sem("tab_init"), 32)
                for t in range(T):
                    pool.wait_ge(sem(f"dest{l}"), t + 1)
                    for k in range(TOPK):
                        g.indirect_dma_start(tabd[l], offsets(dsti[:, t, k:k + 1]), PAY[:, t, k, :], None,
                                             bounds_check=P * BLOCKS - 1, oob_is_err=False).then_inc(sem(f"rows_out{l}"), 16)
                g.memset(HROW[:, 2, :], 0.0).then_inc(sem(f"gix{l}"), 1)
                pool.wait_ge(sem(f"gix{l}"), 1)
                pool.wait_ge(sem("tab_in"), 16 * (l + 1))
                for q in range(2):
                    pool.wait_ge(sem(f"hrow{q}_{l}"), 16 * (T // 2))
                pool.wait_ge(sem(f"meta{l}"), 2)
                nit = pool.value_load(meta[0:1, 0:1], min_val=2, max_val=34)

                def gather(slot):
                    g.indirect_dma_start(HROW[:, slot, :], None, hrows[l], offsets(GIX[:, slot, 0:1]),
                                         bounds_check=T * P - 1, oob_is_err=False).then_inc(sem(f"gath{slot}_{l}"), 16)

                def scatter(slot, rows):
                    g.indirect_dma_start(y6d[l], offsets(SIX[:, slot, 1:2]), rows, None,
                                         bounds_check=TOPK * T * P - 1, oob_is_err=False).then_inc(sem(f"scat{slot}_{l}"), 16)

                for q in range(2):
                    g.tensor_copy(GIX[:, q, :], TAB[:, q, :]).then_inc(sem(f"gix{l}"), 1)
                    pool.wait_ge(sem(f"gix{l}"), q + 2)
                    gather(q)
                for q in range(SLOTS):
                    g.tensor_copy(SIX[:, q, :], TAB[:, BLOCKS - 1, :]).then_inc(sem(f"gix{l}"), 1)
                    pool.wait_ge(sem(f"gix{l}"), q + 4)
                    scatter(q, arena[:, 6144:6144 + D])
                with pool.Fori(0, nit) as i:
                    for b in range(SLOTS):
                        q = (b + 2) % SLOTS
                        pool.wait_ge(sem(f"rows_T{l}"), i * SLOTS + (b + 1))
                        pool.sem_inc(sem("passed"), 1)
                        g.tensor_copy(GIX[:, q, :], TAB[:, bass.ds(i * SLOTS + (b + 2), 1), :].rearrange("p o w -> p (o w)")
                                      ).then_inc(sem(f"gix{l}"), 1)
                        pool.wait_ge(sem(f"gix{l}"), i * SLOTS + (b + 7))
                        pool.sem_inc(sem("passed"), 1)
                        gather(q)
                        pool.wait_ge(sem(f"scat{b}_{l}"), i * 16 + 16)
                        pool.sem_inc(sem("passed"), 1)
                        g.tensor_copy(SIX[:, b, :], TAB[:, bass.ds(i * SLOTS + b, 1), :].rearrange("p o w -> p (o w)")
                                      ).then_inc(sem(f"six{l}"), 1)
                        pool.wait_ge(sem(f"six{l}"), i * SLOTS + (b + 1))
                        pool.wait_ge(sem(f"y_a{l}"), i * SLOTS + (b + 2))
                        pool.wait_ge(sem(f"y_d{l}"), i * SLOTS + (b + 2))
                        pool.sem_inc(sem("passed"), 1)
                        scatter(b, YB[:, b, :])
                pool.wait_ge(sem(f"gath0_{l}"), nit * 16 + 16)
                pool.wait_ge(sem(f"gath1_{l}"), nit * 16 + 16)
                pool.wait_ge(sem(f"gath2_{l}"), nit * 16)
                pool.sem_inc(sem(f"gathers_done{l}"), 1)


_OUT = (P, KC, LAT)


def _constants():
    c = np.zeros((P, NCON), np.float32)

    def put(name, a):
        at, w = CON[name]
        c[:, at:at + w] = a

    i = np.arange(P)
    put("ident", np.eye(P))
    perm = np.zeros((P, P))
    for j in range(P):
        if j % ROPE < ROPE // 2:
            perm[j + ROPE // 2, j] = -1.0
        else:
            perm[j - ROPE // 2, j] = 1.0
    put("perm", perm)
    put("headavg", (i[:, None] // DV_R == i[None, :] // DV_R) / DV_R)
    put("tri", i[:, None] < i[None, :])
    put("headmask", i[:, None] // DK_R == np.arange(HEADS_R)[None, :])
    put("inv1024", 1.0 / 1024)
    put("inv256", 1.0 / 256)
    put("inv128", 1.0 / 128)
    put("ones", 1.0)
    half = ROPE // 2
    nf = ROPE // 4
    inv = (np.float32(10000.0) ** (-np.arange(nf, dtype=np.float32) / np.float32(nf))).astype(np.float32)
    t = np.arange(LAT)
    pr_, pc = (t // 64).astype(np.float32), (t % 64).astype(np.float32)
    ang = np.concatenate([pr_[:, None] * inv, pc[:, None] * inv], -1).astype(np.float32)
    put("cos", np.cos(ang).T[i % half])
    put("sin", np.sin(ang).T[i % half])
    put("iota64", np.arange(EXPERTS)[None])
    put("iota128", np.arange(P)[None])
    put("fold4", i[:, None] % ROPE == np.arange(ROPE)[None])
    put("fold", i[:, None] % EXPERTS == np.arange(EXPERTS)[None])
    d = (np.arange(STRIP_A)[None, :] - 384 - i[:, None]).astype(np.float32)
    pay = np.zeros((LAYERS, P, 6, TOPK, 4), np.int32)
    tok = np.arange(6)[None, :, None] * P + i[:, None, None]
    for l in range(LAYERS):
        pay[l, ..., 0] = tok
        pay[l, ..., 1] = tok + np.arange(TOPK)[None, None, :] * (Plan(l).t_out * P)
    return c, d, pay


def kernel(**inputs):
    import concourse.bacc as _bacc
    from concourse.bass_utils import run_bass_kernel_spmd as _run

    a = {k: np.asarray(v) for k, v in inputs.items()}
    L = LAYERS

    def blocks(w):
        k, n = w.shape
        return w.reshape(k // P, P, n // P, P).transpose(2, 1, 0, 3)

    def chunks(v):
        return v.reshape(-1, P).T

    con, dtab, pay = _constants()
    x = np.concatenate([a["x"][0], a["ctx"]] if a["ctx"].ndim == 2 else [a["x"][0], a["ctx"][0]], 0)
    xT = np.ascontiguousarray(x.T.reshape(KC, P, TOK).transpose(1, 0, 2))
    cc = np.ascontiguousarray(np.stack([a["c"][0], a["c_ctx"]], -1).reshape(KC, P, 2).transpose(1, 0, 2))
    par = np.zeros((L, P, NPAR), np.float32)
    wblk = np.zeros((L, 11, P, 2, KC, P), np.float32)
    order = [0, 2, 1, 3, 4, 5, 6, 7, 8, 9, 10, 11, 12, 13]
    for l in range(L):
        def put(name, v):
            at, w = PAR[name]
            par[l, :, at:at + w] = v
        put("mod_b", np.repeat(chunks(a["mod_b"][l]), 2, 1))
        put("n1", np.repeat(chunks(a["norm1_w"][l]), 2, 1))
        put("n2", np.repeat(chunks(a["norm2_w"][l]), 2, 1))
        put("conv_w", a["conv_w"][l].reshape(CK, 2, P).transpose(2, 1, 0).reshape(P, 2 * CK))
        put("conv_b", chunks(a["conv_b"][l]))
        put("ln_w", chunks(a["conv_ln_w"][l]))
        put("ln_b", chunks(a["conv_ln_b"][l]))
        put("gn_w", chunks(a["ret_gn_w"][l]))
        put("qn", chunks(a["q_norm_w"][l]))
        put("kvn", chunks(a["kv_norm_w"][l]))
        put("decay", a["ret_decay_logit"][l].reshape(1, 8))
        put("router_b", a["router_b"][l][None])
        put("router_w", a["router_w"][l].reshape(KC, P, EXPERTS).transpose(1, 0, 2).reshape(P, -1))
        put("final", chunks(a["final_norm_w"]))
        w = np.zeros((D, 14 * P), np.float32)
        w[:, :a["w_in"].shape[2]] = a["w_in"][l]
        wblk[l, 0:7] = blocks(w)[order].reshape(7, 2, P, KC, P).transpose(0, 2, 1, 3, 4)
        wblk[l, 7:11] = blocks(a["w_out"][l]).reshape(4, 2, P, KC, P).transpose(0, 2, 1, 3, 4)
    uq = a["w_uq"].reshape(L, 2, P, HEADS, QK)
    wuq = np.ascontiguousarray(np.concatenate(
        [uq[..., :NOPE].reshape(L, 2, P, -1), uq[..., NOPE:].reshape(L, 2, P, -1)], -1).transpose(0, 2, 1, 3))
    ukv = a["w_ukv"].reshape(L, P, HEADS, NOPE + DV)
    wukv = np.ascontiguousarray(np.concatenate([ukv[..., :NOPE].reshape(L, P, -1), ukv[..., NOPE:].reshape(L, P, -1)], -1))

    def expert(gate, up, down):
        n = gate.shape[0]
        gu = np.concatenate([gate.reshape(n, KC, P, FE), up.reshape(n, KC, P, FE)], -1).transpose(0, 2, 1, 3)
        dn = down.reshape(n, FE // P, P, D).transpose(0, 2, 1, 3)
        return np.concatenate([gu.reshape(n, P, -1), dn.reshape(n, P, -1)], -1)

    experts = expert(a["exp_w_gate"].reshape(-1, D, FE), a["exp_w_up"].reshape(-1, D, FE), a["exp_w_down"].reshape(-1, FE, D))
    shared = expert(a["sh_w_gate"], a["sh_w_up"], a["sh_w_down"])
    arrays = {"con": con, "cc": cc, "par": par, "xT": xT, "pay": pay, "dtab": dtab,
              "wblk": wblk.reshape(L, 11, P, 2, D), "mod_w": np.ascontiguousarray(a["mod_w"]), "wuq": wuq, "wukv": wukv, "shared": shared, "experts": experts}
    nc = _bacc.Bacc("TRN2", target_bir_lowering=False, num_devices=1)
    A = {k: nc.dram_tensor(f"in_{k}", v.shape, I32 if v.dtype == np.int32 else F32, kind="ExternalInput").ap()
         for k, v in arrays.items()}
    out = nc.dram_tensor("out_0", _OUT, F32, kind="ExternalOutput").ap()
    hybrid_backbone(nc, A, out)
    r = _run(nc, [{f"in_{k}": v for k, v in arrays.items()}], core_ids=[0])
    o = r.results[0]["out_0"]
    return np.ascontiguousarray(o.transpose(2, 1, 0).reshape(1, LAT, D))
```
